# Optimizing a Trainium2 kernel written in Bass

```python
import jax, jax.numpy as jnp
from jax import lax
import numpy as np

D_MODEL = 2048
BATCH = 1
SEQ = 256
DEPTH = 2

N_MIXERS = 2
N_HEADS = 16
HEAD_DIM = D_MODEL // N_HEADS
Q_BLOCK = 128
CONV_WIDTH = 3
D_FF = 4 * D_MODEL
N_MOD = 6
RMS_EPS = 1e-6
FORGET_BIAS_CENTER = 3.0

kernel_name = 'fox_shortconv_hybrid_adaln'

def rmsnorm(x, gain):
    xf = x.astype(jnp.float32)
    inv = lax.rsqrt(jnp.mean(xf * xf, axis=-1, keepdims=True) + RMS_EPS)
    return (xf * inv).astype(x.dtype) * gain

def modulate(h, shift, scale):
    return h * (1.0 + scale[:, None, :]) + shift[:, None, :]

def fox_attention(q, k, v, log_f):
    B, H, S, Dh = q.shape
    nb = S // Q_BLOCK
    F = jnp.cumsum(log_f.astype(jnp.float32), axis=-1)
    q_blocks = q.reshape(B, H, nb, Q_BLOCK, Dh).transpose(2, 0, 1, 3, 4)
    F_blocks = F.reshape(B, H, nb, Q_BLOCK).transpose(2, 0, 1, 3)
    k_pos = jnp.arange(S)
    scale = HEAD_DIM ** -0.5

    def one_block(args):
        blk, q_i, F_i = args
        s = jnp.einsum('bhqd,bhkd->bhqk', q_i, k).astype(jnp.float32) * scale
        s = s + F_i[..., :, None] - F[..., None, :]
        q_pos = blk * Q_BLOCK + jnp.arange(Q_BLOCK)
        causal = k_pos[None, :] <= q_pos[:, None]
        s = jnp.where(causal, s, -jnp.inf)
        p = jax.nn.softmax(s, axis=-1)
        return jnp.einsum('bhqk,bhkd->bhqd', p.astype(v.dtype), v)

    out = lax.map(one_block, (jnp.arange(nb), q_blocks, F_blocks))
    return out.transpose(1, 2, 0, 3, 4).reshape(B, H, S, Dh)

def fox_mixer(h, w_in, b_f, w_out):
    B, S, D = h.shape
    proj = h @ w_in
    q, k, v, f_logit = jnp.split(proj, [D, 2 * D, 3 * D], axis=-1)
    to_heads = lambda t: t.reshape(B, S, N_HEADS, HEAD_DIM).transpose(0, 2, 1, 3)
    log_f = jax.nn.log_sigmoid((f_logit + b_f).astype(jnp.float32)).transpose(0, 2, 1)
    o = fox_attention(to_heads(q), to_heads(k), to_heads(v), log_f)
    o = o.transpose(0, 2, 1, 3).reshape(B, S, D)
    return o @ w_out

def short_conv_mixer(h, w_in, conv_w, w_out):
    S = h.shape[1]
    proj = h @ w_in
    b_gate, c_gate, u = jnp.split(proj, 3, axis=-1)
    u = c_gate * u
    u_pad = jnp.pad(u, ((0, 0), (CONV_WIDTH - 1, 0), (0, 0)))
    y = sum(conv_w[tap] * u_pad[:, tap:tap + S, :] for tap in range(CONV_WIDTH))
    return (b_gate * y) @ w_out

def sq_relu_mlp(h, w_up, w_down):
    return jnp.square(jax.nn.relu(h @ w_up)) @ w_down

def setup_inputs(seed: int = 0) -> dict:
    key = jax.random.key(seed)
    ks = jax.random.split(key, 16)
    D = D_MODEL
    n_fox = (DEPTH + 1) // 2
    n_conv = DEPTH // 2
    nrm = lambda k, shape, fan_in, mult=1.0: jax.random.normal(k, shape, jnp.float32) * (mult * fan_in ** -0.5)
    return {
        'x': jax.random.normal(ks[0], (BATCH, SEQ, D), jnp.float32),
        'c': jax.random.normal(ks[1], (BATCH, D), jnp.float32),
        'ada_w': nrm(ks[2], (DEPTH, D, N_MOD * D), D, 0.5),
        'ada_b': 0.01 * jax.random.normal(ks[3], (DEPTH, N_MOD * D), jnp.float32),
        'norm_mix': 1.0 + 0.02 * jax.random.normal(ks[4], (DEPTH, D), jnp.float32),
        'norm_mlp': 1.0 + 0.02 * jax.random.normal(ks[5], (DEPTH, D), jnp.float32),
        'fox_w_in': nrm(ks[6], (n_fox, D, 3 * D + N_HEADS), D),
        'fox_b_f': FORGET_BIAS_CENTER + 0.1 * jax.random.normal(ks[7], (n_fox, N_HEADS), jnp.float32),
        'fox_w_out': nrm(ks[8], (n_fox, D, D), D),
        'conv_w_in': nrm(ks[9], (n_conv, D, 3 * D), D),
        'conv_w': nrm(ks[10], (n_conv, CONV_WIDTH, D), CONV_WIDTH),
        'conv_w_out': nrm(ks[11], (n_conv, D, D), D),
        'mlp_w_up': nrm(ks[12], (DEPTH, D, D_FF), D),
        'mlp_w_down': nrm(ks[13], (DEPTH, D_FF, D), D_FF),
        'final_norm': 1.0 + 0.02 * jax.random.normal(ks[14], (D,), jnp.float32),
    }

def reference(x, c, ada_w, ada_b, norm_mix, norm_mlp, fox_w_in, fox_b_f, fox_w_out,
              conv_w_in, conv_w, conv_w_out, mlp_w_up, mlp_w_down, final_norm):
    c_act = jax.nn.silu(c)
    for i in range(DEPTH):
        mod = c_act @ ada_w[i] + ada_b[i]
        sh_mix, sc_mix, g_mix, sh_mlp, sc_mlp, g_mlp = jnp.split(mod, N_MOD, axis=-1)
        h = modulate(rmsnorm(x, norm_mix[i]), sh_mix, sc_mix)
        j = i // N_MIXERS
        if i % N_MIXERS == 0:
            mix = fox_mixer(h, fox_w_in[j], fox_b_f[j], fox_w_out[j])
        else:
            mix = short_conv_mixer(h, conv_w_in[j], conv_w[j], conv_w_out[j])
        x = x + g_mix[:, None, :] * mix
        h = modulate(rmsnorm(x, norm_mlp[i]), sh_mlp, sc_mlp)
        x = x + g_mlp[:, None, :] * sq_relu_mlp(h, mlp_w_up[i], mlp_w_down[i])
    return rmsnorm(x, final_norm)


_drawn_inputs = setup_inputs


def setup_inputs(seed=0):
    import zlib

    import numpy as np

    out = dict(_drawn_inputs(seed))
    spreads = {}
    factors = {'norm_mix': 4.547, 'norm_mlp': 4.27, 'fox_b_f': 64.0, 'final_norm': 7.657}
    for name, (base, spread) in spreads.items():
        noise = np.random.default_rng([zlib.crc32(name.encode()), seed]).standard_normal(out[name].shape)
        drawn = base * np.exp(spread * noise) if base else spread * noise
        out[name] = __import__('jax').numpy.asarray(drawn.astype(out[name].dtype))
    for name, factor in factors.items():
        out[name] = (out[name] * factor).astype(out[name].dtype)
    return out
```

```python
from contextlib import ExitStack

import concourse.bass as bass
from concourse import mybir

F32 = mybir.dt.float32
F32R = mybir.dt.float32r
ACT = mybir.ActivationFunctionType
ALU = mybir.AluOpType
AX = mybir.AxisListType

P = 128
D = 2048
T = 256
H = 16
DH = D // H
FF = 4 * D
NMOD = 6
EPS = 1e-6
SCALE = float(DH) ** -0.5
MASKED = -1.0e30

KC = D // P
TT = T // P
NU = 512
NB = NU // P
NG = D // NU
QK = 4
NQ = KC // QK
SLICES = FF // D
NROW = NMOD * KC
VROWS = 96

U_QKV = 0
U_OUT0 = U_QKV + 3 * NG
U_MLP0 = U_OUT0 + NG
U_CONV = U_MLP0 + 2 * NG * SLICES
U_OUT1 = U_CONV + 3 * NG
U_MLP1 = U_OUT1 + NG
U_END = U_MLP1 + 2 * NG * SLICES
A_START = 2 * NG
A_MLP0 = A_START + U_MLP0
A_CONV = A_MLP0 + NG * SLICES
A_END = 2 * NMOD * NG
RING = 8


def build(nc, x, c, ada_w, ada_b, norm_mix, norm_mlp, fox_w_in, fox_b_f, fox_w_out,
          conv_w_in, conv_w, conv_w_out, mlp_w_up, mlp_w_down, final_norm, out):
    ctx = ExitStack()
    with ctx:
        def sb(name, shape, dt=F32):
            return ctx.enter_context(nc.sbuf_tensor(name, shape, dt))

        def sem(name):
            return ctx.enter_context(nc.semaphore(name))

        with nc.sbuf_tensor("start_ring", [P, RING, QK, NU], F32) as start_ring:
            pass
        h = sb("h", [P, KC, 2, T], F32R)
        mid = sb("mid", [P, KC, 2, T], F32R)
        with ExitStack() as shared:
            def early(name, shape, dt=F32):
                return shared.enter_context(nc.sbuf_tensor(name, shape, dt))

            xrow = early("xrow", [P, TT, D])
            vrow = early("vrow", [VROWS, 4, P])
            upto = early("upto", [P, TT, T])
            wf = early("wf", [P, KC, H])
            wf_hi = early("wf_hi", [P, KC, H], F32R)
            wf_lo = early("wf_lo", [P, KC, H], F32R)
        with ExitStack() as shared:
            var = early("var", [P, T])
            inv = early("inv", [P, T])
            newton = early("newton", [P, T])
            squares = early("squares", [P, 2, T])
        with ExitStack() as shared:
            conv_b = shared.enter_context(nc.sbuf_tensor("conv_b", [P, NB, T], F32))
            conv_c = shared.enter_context(nc.sbuf_tensor("conv_c", [P, NB, T], F32))
            conv_u = shared.enter_context(nc.sbuf_tensor("conv_u", [P, NB, T + 2], F32))
            conv_y = shared.enter_context(nc.sbuf_tensor("conv_y", [P, NB, T], F32))
        qs = sb("qs", [P, NB, 2, T], F32R)
        ks = sb("ks", [P, NB, 2, T], F32R)
        vs = sb("vs", [P, TT, 2, NU], F32R)
        pt_hi = qs[:, :, :, :].rearrange("p j s t -> p (j s t)")[:, 0:NB * 384].rearrange("p (j t) -> p j t", j=NB)
        pt_lo = ks[:, :, :, :].rearrange("p j s t -> p (j s t)")[:, 0:NB * 384].rearrange("p (j t) -> p j t", j=NB)

        xT = sb("xT", [P, KC, T])
        raw = sb("raw", [P, NQ, QK, NU])
        ada_raw = sb("ada_raw", [P, 2, QK, NU])
        w_hi = sb("w_hi", [P, 2, QK, NU], F32R)
        w_lo = sb("w_lo", [P, 2, QK, NU], F32R)
        acc = sb("acc", [P, 2, NU])
        scratch = sb("scratch", [P, 2, NB * T])
        tmp = scratch[:, 0, :].rearrange("p (j t) -> p j t", j=NB)
        fsum = scratch[:, 1, :].rearrange("p (j t) -> p j t", j=NB)
        flat = scratch[:, :, :].rearrange("p s n -> p (s n)")
        prob0 = flat[:, 0:NB * P].rearrange("p (j t) -> p j t", j=NB)
        prob1 = flat[:, NB * P:NB * P * 3].rearrange("p (j t) -> p j t", j=NB)

        ident = sb("ident", [P, P])
        ident_r = sb("ident_r", [P, P], F32R)
        causal = sb("causal", [P, P], F32R)
        ones = sb("ones", [P, P])
        ones_r = sb("ones_r", [2, P], F32R)
        vcol = sb("vcol", [P, 4, VROWS])
        ca = sb("ca", [P, KC])
        ce = sb("ce", [P, 2, KC])
        mod = sb("mod", [P, 2 * NROW])
        gain = sb("gain", [P, KC])
        bf = sb("bf", [P, H])
        fz = sb("fz", [P, TT, H])
        fe = sb("fe", [P, TT, H])
        log_f = sb("log_f", [P, TT, H])
        f_tok = sb("f_tok", [P, TT, H])
        nf_hi = sb("nf_hi", [H, T], F32R)
        nf_lo = sb("nf_lo", [H, T], F32R)
        nf_row = sb("nf_row", [2, NB, T], F32R)
        row_max = sb("row_max", [P, TT, NB])
        exp_bias = sb("exp_bias", [P, TT, NB])
        row_sum = sb("row_sum", [P, TT, NB])
        row_inv = sb("row_inv", [P, TT, NB])

        nf_dram = nc.dram_tensor("nf_dram", (2, H, T), F32, kind="Internal").ap()

        ps = ctx.enter_context(nc.psum_tensor("ps", [P, 8, NU], F32))

        C_COL = vcol[:, 0, 0:KC]
        MIX_GAIN = [vcol[:, 0, KC * (1 + l):KC * (2 + l)] for l in range(2)]
        MLP_GAIN = [vcol[:, 0, KC * (3 + l):KC * (4 + l)] for l in range(2)]
        FINAL = vcol[:, 0, KC * 5:KC * 6]
        ada_bias = vcol[:, 1:3, :].rearrange("p a n -> p (a n)")
        taps = vcol[:, 3, 0:3 * KC]

        x_arrived = sem("x_arrived")
        vec_arrived = sem("vec_arrived")
        wf_arrived = sem("wf_arrived")
        start_arrived = [sem(f"start_arrived{i}") for i in range(RING)]
        raw_arrived = [sem(f"raw_arrived{i}") for i in range(NQ)]
        ada_arrived = [sem(f"ada_arrived{i}") for i in range(2)]
        nf_arrived = sem("nf_arrived")
        nf_stored = sem("nf_stored")
        out_written = sem("out_written")
        const_ready = sem("const_ready")
        vec_turned = sem("vec_turned")
        vec_ready = sem("vec_ready")
        c_exp = sem("c_exp")
        c_step = sem("c_step")
        x_turned = sem("x_turned")
        hi_ready = sem("hi_ready")
        split_ready = sem("split_ready")
        split_used = sem("split_used")
        unit_done = sem("unit_done")
        half_ready = sem("half_ready")
        evacuated = sem("evacuated")
        ada_steps = sem("ada_steps")
        ada_summed = sem("ada_summed")
        mod_ready = sem("mod_ready")
        squared = sem("squared")
        var_ready = sem("var_ready")
        conv_zero = sem("conv_zero")
        reduced = sem("reduced")
        normed = sem("normed")
        norm_step = sem("norm_step")
        root_ready = sem("root_ready")
        scaled = sem("scaled")
        modulated = sem("modulated")
        h_hi = sem("h_hi")
        h_ready = sem("h_ready")
        f_split = sem("f_split")
        f_lo = sem("f_lo")
        f_done = sem("f_done")
        f_step = sem("f_step")
        f_act = sem("f_act")
        f_rows = sem("f_rows")
        nf_ready = sem("nf_ready")
        qkv_hi = sem("qkv_hi")
        qkv_ready = sem("qkv_ready")
        scores_done = sem("scores_done")
        max_step = sem("max_step")
        exp_done = sem("exp_done")
        norm_p = sem("norm_p")
        turned = sem("turned")
        pt_hi_ready = sem("pt_hi_ready")
        pt_ready = sem("pt_ready")
        pv_done = sem("pv_done")
        attn_hi = sem("attn_hi")
        attn_ready = sem("attn_ready")
        gated = sem("gated")
        added = sem("added")
        relu2 = sem("relu2")
        hid_hi = sem("hid_hi")
        hid_ready = sem("hid_ready")
        conv_in = sem("conv_in")
        conv_tap = sem("conv_tap")
        conv_step = sem("conv_step")
        conv_gated = sem("conv_gated")
        conv_hi = sem("conv_hi")
        conv_ready = sem("conv_ready")
        out_turned = sem("out_turned")
        out_copied0 = sem("out_copied0")
        out_copied1 = sem("out_copied1")

        block = ctx.enter_context(nc.Block())

        def ds(start, size):
            return bass.ds(start, size)

        def quarter(w, row0, q, col, width=NU):
            return w.rearrange("(k p) n -> p k n", p=P)[:, ds(row0 + QK * q, QK), ds(col, width)]

        def ada_quarter(a_layer, n, q):
            return quarter(ada_w[a_layer], 0, q, NU * n)

        @block.sync
        def _(sp):
            sp.dma_start(vrow[0:KC, 0, :], c.rearrange("b (k p) -> (b k) p", p=P)).then_inc(vec_arrived, 16)
            sp.dma_start(vrow[KC:3 * KC, 0, :], norm_mix.rearrange("l (k p) -> (l k) p", p=P)).then_inc(vec_arrived, 16)
            sp.dma_start(vrow[3 * KC:5 * KC, 0, :], norm_mlp.rearrange("l (k p) -> (l k) p", p=P)).then_inc(vec_arrived, 16)
            sp.dma_start(vrow[5 * KC:6 * KC, 0, :], final_norm.rearrange("(k p) -> k p", p=P)).then_inc(vec_arrived, 16)
            for l in range(2):
                sp.dma_start(vrow[:, 1 + l, :], ada_b[l].rearrange("(k p) -> k p", p=P)).then_inc(vec_arrived, 16)
            sp.dma_start(vrow[0:3 * KC, 3, :], conv_w[0].rearrange("a (k p) -> (a k) p", p=P)).then_inc(vec_arrived, 16)
            sp.dma_start(xrow[:, :, :], x[0].rearrange("(a p) n -> p a n", p=P)).then_inc(x_arrived, 16)
            sp.dma_start(wf[:, :, :], fox_w_in[0].rearrange("(k p) n -> p k n", p=P)[:, :, 3 * D:3 * D + H]).then_inc(wf_arrived, 16)
            sp.dma_start(bf[:, :], fox_b_f.broadcast_to([P, H])).then_inc(wf_arrived, 16)

            def unit(u, w, row0, col):
                for q in range(NQ):
                    sp.wait_ge(split_ready, NQ * u + q + 1)
                    sp.dma_start(raw[:, q], quarter(w, row0, q, col)).then_inc(raw_arrived[q], 16)

            def mlp(l, base):
                with sp.Fori(0, SLICES) as s:
                    for n in range(NG):
                        unit(base + 2 * NG * s + n, mlp_w_up[l], 0, D * s + NU * n)
                    for n in range(NG):
                        unit(base + 2 * NG * s + NG + n, mlp_w_down[l], KC * s, NU * n)

            with sp.Fori(0, NG) as g:
                for part in range(3):
                    unit(U_QKV + 3 * g + part, fox_w_in[0], 0, D * part + NU * g)
            with sp.Fori(0, NG) as n:
                unit(U_OUT0 + n, fox_w_out[0], 0, NU * n)
            mlp(0, U_MLP0)
            with sp.Fori(0, NG) as g:
                for part in range(3):
                    unit(U_CONV + 3 * g + part, conv_w_in[0], 0, D * part + NU * g)
            with sp.Fori(0, NG) as n:
                unit(U_OUT1 + n, conv_w_out[0], 0, NU * n)
            mlp(1, U_MLP1)
            for m in range(NG):
                sp.wait_ge(out_copied0, m + 1)
                sp.wait_ge(out_copied1, m + 1)
                sp.dma_start(out[0].rearrange("(a p) n -> p a n", p=P)[:, :, NU * m:NU * (m + 1)],
                             raw[:, m, 0:TT, :]).then_inc(out_written, 16)
            sp.wait_ge(out_written, 16 * NG)

        @block.gpsimd
        def _(pool):
            for n in range(RING):
                pool.dma_start(start_ring[:, n], ada_quarter(0, n // NQ, n % NQ)).then_inc(start_arrived[n], 16)
            pool.memset(ident[:, :], 0.0).then_inc(const_ready, 1)
            pool.memset(ident_r[:, :].bitcast(F32), 0.0).then_inc(const_ready, 1)
            pool.memset(causal[:, :].bitcast(F32), 0.0).then_inc(const_ready, 1)
            pool.memset(upto[:, :, :], 1.0).then_inc(const_ready, 1)
            pool.memset(ones[:, :], 1.0).then_inc(const_ready, 1)
            pool.memset(ones_r[:, :].bitcast(F32), 1.0).then_inc(const_ready, 1)
            pool.wait_ge(const_ready, 6)
            for m in (ident, ident_r):
                pool.affine_select(out=m[:, :], in_=m[:, :].bitcast(F32), compare_op=ALU.not_equal, fill=1.0,
                                   base=0, pattern=[[-1, P]], channel_multiplier=1).then_inc(const_ready, 1)
            pool.affine_select(out=causal[:, :], in_=causal[:, :].bitcast(F32), compare_op=ALU.is_ge, fill=MASKED,
                               base=0, pattern=[[-1, P]], channel_multiplier=1).then_inc(const_ready, 1)
            for a in range(TT):
                pool.affine_select(out=upto[:, a, :], in_=upto[:, a, :], compare_op=ALU.is_ge, fill=0.0,
                                   base=-P * a, pattern=[[1, T]], channel_multiplier=-1).then_inc(const_ready, 1)
            with pool.Fori(1, A_START * NQ // RING) as r:
                for n in range(RING):
                    pool.wait_ge(ada_steps, QK * (RING * r + n - RING + 1))
                    pool.dma_start(start_ring[:, n], ada_quarter(0, (RING // NQ) * r + n // NQ, n % NQ)
                                   ).then_inc(start_arrived[n], 16)

            def ada_units(layer, first, a0, a1):
                with pool.Fori(a0, a1) as a:
                    for q in range(NQ):
                        if first is None or q >= 2:
                            pool.wait_ge(ada_steps, KC * a + QK * (q - 1))
                        pool.dma_start(ada_raw[:, q % 2], ada_quarter(layer, a - NMOD * NG * layer, q)
                                       ).then_inc(ada_arrived[q % 2], 16)

            ada_units(0, 1, A_START, A_START + 1)
            ada_units(0, None, A_START + 1, NMOD * NG)
            ada_units(1, None, NMOD * NG, A_END)

        @block.tensor
        def _(pe):
            mm = nc.tensor.matmul

            def multiply(u, par, rhs, ada=None, tokens_out=False):
                pe.wait_ge(evacuated, u + 1)
                for q in range(NQ):
                    pe.wait_ge(split_ready, NQ * u + q + NQ + 1)
                    last = None
                    for kk in range(QK):
                        k = QK * q + kk
                        hi, lo = w_hi[:, q % 2, kk, :], w_lo[:, q % 2, kk, :]
                        if tokens_out:
                            for a in range(TT):
                                o = ps[:, NB * par + a, :]
                                xh, xl = rhs[:, k, 0, P * a:P * (a + 1)], rhs[:, k, 1, P * a:P * (a + 1)]
                                mm(o, xh, hi, start=(k == 0), stop=False)
                                mm(o, xl, hi, start=False, stop=False)
                                last = mm(o, xh, lo, start=False, stop=(k == KC - 1))
                        else:
                            for j in range(NB):
                                cols = slice(P * j, P * (j + 1))
                                mm(ps[:, NB * par + j, :], hi[:, cols], rhs[:, k, :, :].rearrange("p s t -> p (s t)"),
                                   start=(k == 0), stop=False)
                                last = mm(ps[:, NB * par + j, 0:T], lo[:, cols], rhs[:, k, 0, :],
                                          start=False, stop=(k == KC - 1))
                    last.then_inc(split_used, 1)
                    if q == 1 and ada is not None:
                        pe.wait_ge(evacuated, u + 2)
                        ada_sum(*ada, NB * (1 - par))

            def ada_sum(a, slot, bank):
                pe.wait_ge(ada_steps, KC * (a + 1))
                for j in range(NB):
                    last = mm(ps[:, bank, j:j + 1], acc[:, slot, P * j:P * (j + 1)], ones[:, 0:1],
                              start=True, stop=True)
                last.then_inc(ada_summed, 1)

            def norm_sum(i):
                for m in range(NQ):
                    pe.wait_ge(reduced, NQ * i + m + 1)
                    last = mm(ps[:, 0, 0:T], ones[:, :], squares[:, m % 2, :], start=(m == 0), stop=(m == NQ - 1))
                    last.then_inc(normed, 1)

            pe.wait_ge(const_ready, 11)
            pe.wait_ge(vec_arrived, 16 * 7)
            for i in range(4):
                rows = 3 * KC if i == 3 else VROWS
                last = nc.tensor.transpose(ps[:, 7, VROWS * i:VROWS * i + rows], vrow[0:rows, i, :], ident[0:rows, 0:rows])
            last.then_inc(vec_turned, 1)
            pe.wait_ge(x_arrived, 16)
            for half in range(2):
                if half == 1:
                    pe.wait_ge(vec_ready, 1)
                for k in range(8):
                    for a in range(TT):
                        last = nc.tensor.transpose(
                            ps[:, NB * half + k // 2, T * (k % 2) + P * a:T * (k % 2) + P * (a + 1)],
                            xrow[:, a, P * (8 * half + k):P * (8 * half + k + 1)], ident[:, :])
                last.then_inc(x_turned, 1)
            pe.wait_ge(evacuated, 2)
            with pe.Fori(0, A_START // 2) as r:
                for i in range(2):
                    if i == 0:
                        pe.wait_ge(mod_ready, 2 * r)
                    ada_sum(2 * r + i, i, NB * i)

            def wait_h(i, q):
                pe.wait_ge(h_ready, NQ * i + q + 1)

            norm_sum(0)
            pe.wait_ge(h_ready, NQ)
            pe.wait_ge(f_lo, 1)
            for a in range(TT):
                for k in range(KC):
                    o = ps[:, NB, H * a:H * (a + 1)]
                    xh, xl = h[:, k, 0, P * a:P * (a + 1)], h[:, k, 1, P * a:P * (a + 1)]
                    mm(o, xh, wf_hi[:, k, :], start=(k == 0), stop=False)
                    mm(o, xl, wf_hi[:, k, :], start=False, stop=False)
                    last = mm(o, xh, wf_lo[:, k, :], start=False, stop=(k == KC - 1))
            last.then_inc(f_done, 1)
            pe.wait_ge(f_step, 3)
            for a in range(TT):
                mm(ps[0:H, NB + 1, 0:T], log_f[:, a, :], upto[:, a, :], start=(a == 0), stop=(a == TT - 1))
            for b in range(TT):
                for a in range(TT):
                    last = mm(ps[:, NB + 2, H * b:H * (b + 1)], upto[:, a, P * b:P * (b + 1)], log_f[:, a, :],
                              start=(a == 0), stop=(a == TT - 1))
            last.then_inc(f_done, 1)
            pe.wait_ge(f_rows, 2)

            def attend(g, par):
                s_bank, t_bank = NB * par, NB * (1 - par)
                pe.wait_ge(qkv_ready, 2 * g + 2)
                pe.wait_ge(evacuated, 3 * g + 2 + 3)
                pe.wait_ge(nf_arrived, 16 * g + 16)
                for j in range(NB):
                    for b in range(TT):
                        n = P * (b + 1)
                        o = ps[:, s_bank + j, P * b:P * b + n]
                        qh, ql = qs[:, j, 0, P * b:P * (b + 1)], qs[:, j, 1, P * b:P * (b + 1)]
                        mm(o, qh, ks[:, j, 0, 0:n], start=True, stop=False)
                        mm(o, qh, ks[:, j, 1, 0:n], start=False, stop=False)
                        mm(o, ql, ks[:, j, 0, 0:n], start=False, stop=False)
                        mm(o, ones_r[:, :], nf_row[:, j, 0:n], start=False, stop=False)
                        last = mm(o[:, n - P:n], ident_r[:, :], causal[:, :], start=False, stop=True)
                last.then_inc(scores_done, 1)
                pe.wait_ge(norm_p, 3 * g + 3)
                for j in range(NB):
                    nc.tensor.transpose(ps[:, t_bank + j, 0:P], prob0[:, j, :], ident[:, :])
                    for b in range(TT):
                        last = nc.tensor.transpose(ps[:, t_bank + j, P * (b + 1):P * (b + 2)],
                                                   prob1[:, j, P * b:P * (b + 1)], ident[:, :])
                last.then_inc(turned, 1)
                pe.wait_ge(pt_ready, g + 1)
                for j in range(NB):
                    o = ps[:, s_bank + j, 0:T]
                    for b, part, dst in ((0, slice(0, T), o), (1, slice(T, T + P), o[:, P:T])):
                        vh, vl = vs[:, b, 0, P * j:P * (j + 1)], vs[:, b, 1, P * j:P * (j + 1)]
                        mm(dst, vh, pt_hi[:, j, part], start=(b == 0), stop=False)
                        mm(dst, vh, pt_lo[:, j, part], start=False, stop=False)
                        last = mm(dst, vl, pt_hi[:, j, part], start=False, stop=(b == 1))
                last.then_inc(pv_done, 1)
                pe.wait_ge(attn_ready, g + 1)

            def mod_read(a):
                pe.wait_ge(mod_ready, a + 2)

            with pe.Fori(0, NG // 2) as r:
                for i in range(2):
                    for t in range(3):
                        pos = 3 * i + t
                        u = 6 * r + pos
                        multiply(u, pos % 2, h, (u + A_START - 1, (pos + 1) % 2), tokens_out=(t == 2))
                        mod_read(u + A_START - 1)
                    attend(2 * r + i, (3 * i + 3) % 2)
            with pe.Fori(0, NG // 2) as r:
                for i in range(2):
                    u = U_OUT0 + 2 * r + i
                    multiply(u, i, mid, (u + A_START - 1, (i + 1) % 2))
                    mod_read(u + A_START - 1)
            ada_sum(A_MLP0 - 1, 1, 0)
            mod_read(A_MLP0 - 1)

            def mlp(base, i, adas):
                norm_sum(i)
                with pe.Fori(0, SLICES) as s:
                    for n in range(NG):
                        if n == 0:
                            pe.wait_ge(h_ready, NQ * i + NQ)
                        u = base + 2 * NG * s + n
                        a = A_MLP0 + NG * s + n // 2
                        multiply(u, n % 2, h, (a, (n // 2) % 2) if adas and n % 2 else None)
                        if adas and n % 2:
                            mod_read(a)
                    pe.wait_ge(hid_ready, (SLICES * (i // 2) + s + 1) * NG)
                    for n in range(NG):
                        u = base + 2 * NG * s + NG + n
                        a = A_MLP0 + NG * s + NG // 2 + n // 2
                        multiply(u, n % 2, mid, (a, (n // 2) % 2) if adas and n % 2 else None)
                        if adas and n % 2:
                            mod_read(a)

            mlp(U_MLP0, 1, True)
            norm_sum(2)
            pe.wait_ge(h_ready, 3 * NQ)
            with pe.Fori(0, NG // 2) as r:
                for i in range(2):
                    for t in range(3):
                        pos = 3 * i + t
                        a = A_CONV + 4 * r + 2 * i + t - 1
                        multiply(U_CONV + 6 * r + pos, pos % 2, h, (a, (t + 1) % 2) if t else None)
                        if t:
                            mod_read(a)
            pe.wait_ge(conv_ready, NG)
            with pe.Fori(0, NG // 2) as r:
                for i in range(2):
                    multiply(U_OUT1 + 2 * r + i, i, mid)
            mlp(U_MLP1, 3, False)
            norm_sum(4)
            for m in range(NG):
                pe.wait_ge(modulated, 4 * NQ * QK + QK * (m + 1))
                if m >= 2:
                    pe.wait_ge(out_copied0, m - 1)
                    pe.wait_ge(out_copied1, m - 1)
                for a in range(TT):
                    for j in range(NB):
                        last = nc.tensor.transpose(ps[:, NB + 2 * (m % 2) + a, P * j:P * (j + 1)],
                                                   scratch[:, m % 2, T * j + P * a:T * j + P * (a + 1)], ident[:, :])
                last.then_inc(out_turned, 1)

        @block.scalar
        def _(act):
            op = nc.scalar.activation

            def split(u, q, first=False):
                act.wait_ge(raw_arrived[q], 16 * u + 16)
                if not first:
                    act.wait_ge(split_used, NQ * u + q - 1)
                op(w_hi[:, q % 2], raw[:, q], ACT.Copy).then_inc(hi_ready, 1)

            def body(u, evac, more=True):
                split(u, 2)
                split(u, 3)
                if more:
                    split(u + 1, 0)
                    split(u + 1, 1)
                act.wait_ge(split_used, NQ * u + NQ)
                evac()

            def half(u, par, scale=1.0):
                act.wait_ge(evacuated, u + 2)
                op(tmp, ps[:, NB * par:NB * (par + 1), T:2 * T], ACT.Copy, scale=scale).then_inc(half_ready, 1)

            def halves(u):
                return u

            def residual(u, par, gate0, k, n_gated):
                half(u, par)
                act.wait_ge(evacuated, u + 3)
                for j in range(NB):
                    last = op(fsum[:, j, :], fsum[:, j, :], ACT.Copy, scale=mod[:, ds(gate0 + k + j, 1)])
                last.then_inc(gated, 1)

            act.wait_ge(vec_ready, 1)
            op(ce[:, 0, :], C_COL, ACT.Exp, scale=-1.0).then_inc(c_exp, 1)
            act.wait_ge(wf_arrived, 32)
            op(wf_hi[:, :, :], wf[:, :, :], ACT.Copy).then_inc(f_split, 1)
            split(0, 0, True)
            split(0, 1, True)

            def norm(i, shift0=None):
                for m in range(NQ):
                    if i:
                        act.wait_ge(added, n_added[i])
                    else:
                        act.wait_ge(evacuated, 2)
                    if m >= 2:
                        act.wait_ge(reduced, NQ * i + m - 1)
                    op(scratch[:, m % 2, :], xT[:, QK * m:QK * (m + 1), :].rearrange("p k t -> p (k t)"),
                       ACT.Square).then_inc(squared, 1)
                act.wait_ge(norm_step, 6 * i + 2)
                op(inv[:, :], newton[:, :], ACT.Sqrt).then_inc(root_ready, 1)
                for m in range(NQ):
                    act.wait_ge(scaled, NQ * i + m + 1)
                    for j in range(QK):
                        k = QK * m + j
                        f = scratch[:, m % 2, T * j:T * (j + 1)]
                        if shift0 is None:
                            op(f, f, ACT.Copy, scale=vcol[:, 0, 5 * KC + k:5 * KC + k + 1]).then_inc(modulated, 1)
                        else:
                            op(f, f, ACT.Identity, scale=gain[:, k:k + 1],
                               bias=mod[:, shift0 + k:shift0 + k + 1]).then_inc(modulated, 1)
                    if shift0 is not None:
                        act.wait_ge(modulated, KC * i + QK * (m + 1))
                        op(h[:, QK * m:QK * (m + 1), 0, :], scratch[:, m % 2, :].rearrange("p (k t) -> p k t", k=QK),
                           ACT.Copy).then_inc(h_hi, 1)

            n_added = [0, NG, NG * (1 + SLICES), NG * (2 + SLICES), 2 * NG * (1 + SLICES)]

            norm(0, 0)
            act.wait_ge(f_step, 2)
            op(fe[:, :, :], fe[:, :, :], ACT.Exp).then_inc(f_act, 1)
            act.wait_ge(f_act, 1)
            op(fe[:, :, :], fe[:, :, :], ACT.Ln, bias=1.0).then_inc(f_act, 1)
            act.wait_ge(f_done, 2)
            op(nf_hi[:, :], ps[0:H, NB + 1, 0:T], ACT.Copy, scale=-1.0).then_inc(f_act, 1)
            act.wait_ge(f_rows, 2)

            def load_nf(g):
                act.dma_start(nf_row[:, :, :].bitcast(F32), nf_dram[:, ds(NB * g, NB), :]).then_inc(nf_arrived, 16)

            act.wait_ge(f_act, 3)
            act.dma_start(nf_dram[0], nf_hi[:, :].bitcast(F32)).then_inc(nf_stored, 16)
            act.dma_start(nf_dram[1], nf_lo[:, :].bitcast(F32)).then_inc(nf_stored, 16)
            act.wait_ge(nf_stored, 32)

            def attend(g, par):
                s_bank, t_bank = NB * par, NB * (1 - par)
                act.wait_ge(max_step, 4 * g + 4)
                for j in range(NB):
                    for b in range(TT):
                        dst = prob0[:, j, :] if b == 0 else prob1[:, j, :]
                        op(dst, ps[:, s_bank + j, P * b:P * b + P * (b + 1)], ACT.Exp, bias=exp_bias[:, b, j:j + 1],
                           accum_out=row_sum[:, b, j:j + 1]).then_inc(exp_done, 1)
                act.wait_ge(turned, g + 1)
                op(pt_hi, ps[:, t_bank:t_bank + NB, 0:T + P], ACT.Copy).then_inc(pt_hi_ready, 1)
                act.wait_ge(pv_done, g + 1)
                op(mid[:, ds(NB * g, NB), 0, :], ps[:, s_bank:s_bank + NB, 0:T], ACT.Copy).then_inc(attn_hi, 1)

            with act.Fori(0, NG // 2) as r:
                for i in range(2):
                    g = 2 * r + i
                    for t in range(3):
                        pos = 3 * i + t
                        u = 6 * r + pos
                        if t == 0:
                            act.wait_ge(scores_done, g)
                            load_nf(g)

                        def evac():
                            if t == 2:
                                op(vs[:, :, 0, :], ps[:, NB * (pos % 2):NB * (pos % 2) + TT, :], ACT.Copy).then_inc(qkv_hi, 1)
                            else:
                                dst = (qs, ks)[t]
                                half(u, pos % 2, SCALE if t == 0 else 1.0)
                                act.wait_ge(evacuated, u + 3)
                                op(dst[:, :, 0, :], fsum, ACT.Copy).then_inc(qkv_hi, 1)
                        body(u, evac)
                    attend(g, (3 * i + 3) % 2)
            with act.Fori(0, NG // 2) as r:
                for i in range(2):
                    n = 2 * r + i
                    body(U_OUT0 + n, lambda: residual(U_OUT0 + n, i, 2 * KC, NB * n, n))

            def mlp_slice(s, base, l, last=False):
                for n in range(NG):
                    u = base + 2 * NG * s + n

                    def evac():
                        half(u, n % 2)
                        act.wait_ge(relu2, SLICES * NG * l + NG * s + n + 1)
                        op(mid[:, NB * n:NB * (n + 1), 0, :], fsum, ACT.Copy).then_inc(hid_hi, 1)
                    body(u, evac)
                for n in range(NG):
                    u = base + 2 * NG * s + NG + n
                    body(u, lambda: residual(u, n % 2, NROW * l + 5 * KC, NB * n, 0), more=not (last and n == NG - 1))

            norm(1, 3 * KC)
            with act.Fori(0, SLICES) as s:
                mlp_slice(s, U_MLP0, 0)
            norm(2, NROW)
            with act.Fori(0, NG // 2) as r:
                for i in range(2):
                    g = 2 * r + i
                    for t in range(3):
                        pos = 3 * i + t
                        u = U_CONV + 6 * r + pos

                        def evac():
                            half(u, pos % 2)
                            if t == 2:
                                act.wait_ge(conv_in, g + 1)
                                act.wait_ge(conv_ready, g)
                                for j in range(NB):
                                    last = op(conv_y[:, j, :], conv_u[:, j, 0:T], ACT.Copy, scale=taps[:, ds(NB * g + j, 1)])
                                last.then_inc(conv_tap, 1)
                                act.wait_ge(conv_gated, g + 1)
                                op(mid[:, ds(NB * g, NB), 0, :], conv_y[:, :, :], ACT.Copy).then_inc(conv_hi, 1)
                        body(u, evac)
            with act.Fori(0, NG // 2) as r:
                for i in range(2):
                    n = 2 * r + i
                    body(U_OUT1 + n, lambda: residual(U_OUT1 + n, i, NROW + 2 * KC, NB * n, n))
            norm(3, NROW + 3 * KC)
            with act.Fori(0, SLICES - 1) as s:
                mlp_slice(s, U_MLP1, 1)
            mlp_slice(SLICES - 1, U_MLP1, 1, last=True)
            norm(4)
            for m in range(NG):
                act.wait_ge(out_turned, m + 1)
                op(raw[:, m, 0, :], ps[:, NB + 2 * (m % 2), :], ACT.Copy).then_inc(out_copied0, 1)

        @block.vector
        def _(dve):
            v = nc.vector

            def split(u, q):
                dve.wait_ge(hi_ready, NQ * u + q + 1)
                v.tensor_tensor(w_lo[:, q % 2], raw[:, q], w_hi[:, q % 2].bitcast(F32), ALU.subtract).then_inc(split_ready, 1)

            def ada_add(a, slot, q, src):
                for kk in range(QK):
                    k = QK * q + kk
                    if k == 0:
                        v.tensor_scalar(acc[:, slot, :], src[:, kk, :], ca[:, 0:1], None, ALU.mult).then_inc(ada_steps, 1)
                    else:
                        dve.wait_ge(ada_steps, KC * a + k)
                        v.scalar_tensor_tensor(acc[:, slot, :], src[:, kk, :], ca[:, k:k + 1], acc[:, slot, :],
                                               ALU.mult, ALU.add).then_inc(ada_steps, 1)

            def ada_store(a, bank, again=1):
                dve.wait_ge(ada_summed, a + 1 + again)
                v.tensor_tensor(mod[:, ds(NB * a, NB)], ps[:, bank, 0:NB], ada_bias[:, ds(NB * a, NB)],
                                ALU.add).then_inc(mod_ready, 1)

            def body(u, evac, ada=None, store=None, more=True):
                for i, (du, q) in enumerate(((0, 2), (0, 3), (1, 0), (1, 1))):
                    if du == 0 or more:
                        split(u + du, q)
                    if i == 1 and store is not None:
                        ada_store(*store)
                    if ada is not None:
                        a, slot = ada
                        if i == 0:
                            dve.wait_ge(ada_summed, a)
                        dve.wait_ge(ada_arrived[i % 2], 16 * (2 * (a - A_START) + i // 2 + 1))
                        ada_add(a, slot, i, ada_raw[:, i % 2])
                evac()

            def whole(u, par, dst, scale=1.0, n_half=None, used=()):
                for wait in used:
                    dve.wait_ge(*wait)
                dve.wait_ge(half_ready, n_half)
                if scale == 1.0:
                    v.tensor_tensor(dst, ps[:, NB * par:NB * (par + 1), 0:T], tmp, ALU.add).then_inc(evacuated, 1)
                else:
                    v.scalar_tensor_tensor(dst, ps[:, NB * par:NB * (par + 1), 0:T], scale, tmp,
                                           ALU.mult, ALU.add).then_inc(evacuated, 1)

            def residual(u, par, k, n_half, n_res, used=()):
                whole(u, par, fsum, n_half=n_half, used=((added, n_res),) + used)
                dve.wait_ge(gated, n_res + 1)
                v.tensor_tensor(xT[:, ds(k, NB), :], xT[:, ds(k, NB), :], fsum, ALU.add).then_inc(added, 1)

            v.memset(gain[:, :], 0.0).then_inc(split_ready, NQ)
            dve.wait_ge(vec_turned, 1)
            v.tensor_copy(vcol[:, 0:3, :], ps[:, 7, 0:3 * VROWS].rearrange("p (a n) -> p a n", a=3)).then_inc(c_step, 1)
            v.tensor_copy(vcol[:, 3, 0:3 * KC], ps[:, 7, 3 * VROWS:3 * VROWS + 3 * KC]).then_inc(vec_ready, 1)
            dve.wait_ge(c_exp, 1)
            dve.wait_ge(c_step, 1)
            v.tensor_scalar(ce[:, 1, :], ce[:, 0, :], 1.0, None, ALU.add).then_inc(c_step, 1)
            dve.wait_ge(c_step, 2)
            v.reciprocal(ce[:, 0, :], ce[:, 1, :]).then_inc(c_step, 1)
            dve.wait_ge(c_step, 3)
            v.tensor_tensor(ca[:, :], C_COL, ce[:, 0, :], ALU.mult).then_inc(c_step, 1)
            for half in range(2):
                dve.wait_ge(x_turned, half + 1)
                v.tensor_copy(xT[:, 8 * half:8 * (half + 1), :],
                              ps[:, NB * half:NB * (half + 1), :].rearrange("p b (k t) -> p (b k) t", k=2)
                              ).then_inc(evacuated, 1)
            dve.wait_ge(c_step, 4)
            with dve.Fori(0, A_START // 2) as r:
                for i in range(2):
                    for q in range(NQ):
                        dve.wait_ge(start_arrived[NQ * i + q], 16 * r + 16)
                        ada_add(2 * r + i, i, q, start_ring[:, NQ * i + q])
                for i in range(2):
                    ada_store(2 * r + i, NB * i, 0)
            dve.wait_ge(f_split, 1)
            v.tensor_tensor(wf_lo[:, :, :], wf[:, :, :], wf_hi[:, :, :].bitcast(F32), ALU.subtract).then_inc(f_lo, 1)
            split(0, 0)
            split(0, 1)

            def norm(i, gains=None, scale0=None, n_mod=None):
                if gains is not None:
                    dve.wait_ge(mod_ready, n_mod)
                    v.scalar_tensor_tensor(gain[:, :], mod[:, scale0:scale0 + KC], 1.0, gains, ALU.add, ALU.mult).then_inc(norm_step, 1)
                else:
                    v.memset(gain[:, :], 0.0).then_inc(norm_step, 1)
                for m in range(NQ):
                    dve.wait_ge(squared, NQ * i + m + 1)
                    if m >= 2:
                        dve.wait_ge(normed, NQ * i + m - 1)
                    v.tensor_reduce(squares[:, m % 2, :], scratch[:, m % 2, :].rearrange("p (k t) -> p t k", k=QK),
                                    AX.X, ALU.add).then_inc(reduced, 1)
                dve.wait_ge(normed, NQ * i + NQ)
                v.tensor_scalar(var[:, :], ps[:, 0, 0:T], 1.0 / D, EPS, ALU.mult, ALU.add).then_inc(var_ready, 1)
                dve.wait_ge(var_ready, i + 1)
                v.reciprocal(newton[:, :], var[:, :]).then_inc(norm_step, 1)
                dve.wait_ge(root_ready, i + 1)
                v.tensor_tensor(newton[:, :], inv[:, :], inv[:, :], ALU.mult).then_inc(norm_step, 1)
                dve.wait_ge(norm_step, 6 * i + 3)
                v.tensor_tensor(newton[:, :], newton[:, :], var[:, :], ALU.mult).then_inc(norm_step, 1)
                dve.wait_ge(norm_step, 6 * i + 4)
                v.tensor_scalar(newton[:, :], newton[:, :], -0.5, 1.5, ALU.mult, ALU.add).then_inc(norm_step, 1)
                dve.wait_ge(norm_step, 6 * i + 5)
                v.tensor_tensor(inv[:, :], inv[:, :], newton[:, :], ALU.mult).then_inc(norm_step, 1)
                dve.wait_ge(norm_step, 6 * i + 6)
                inv_all = inv[:, :].rearrange("p (o t) -> p o t", o=1).broadcast_to([P, QK, T])
                for m in range(NQ):
                    if m >= 2:
                        dve.wait_ge(*((out_turned, m - 1) if gains is None else (h_ready, NQ * i + m - 1)))
                    v.tensor_tensor(scratch[:, m % 2, :].rearrange("p (k t) -> p k t", k=QK),
                                    xT[:, QK * m:QK * (m + 1), :], inv_all, ALU.mult).then_inc(scaled, 1)
                    if gains is not None and m >= 1:
                        low(i, m - 1)
                if gains is not None:
                    low(i, NQ - 1)

            def low(i, m):
                dve.wait_ge(h_hi, NQ * i + m + 1)
                v.tensor_tensor(h[:, QK * m:QK * (m + 1), 1, :], scratch[:, m % 2, :].rearrange("p (k t) -> p k t", k=QK),
                                h[:, QK * m:QK * (m + 1), 0, :].bitcast(F32), ALU.subtract).then_inc(h_ready, 1)

            norm(0, MIX_GAIN[0], KC, A_START)
            dve.wait_ge(h_ready, NQ)
            dve.wait_ge(f_done, 1)
            v.tensor_tensor(fz[:, :, :], ps[:, NB, 0:TT * H].rearrange("p (a h) -> p a h", a=TT),
                            bf[:, :].rearrange("p (o h) -> p o h", o=1).broadcast_to([P, TT, H]), ALU.add).then_inc(f_step, 1)
            dve.wait_ge(f_step, 1)
            v.scalar_tensor_tensor(fe[:, :, :], fz[:, :, :], -1.0, fz[:, :, :], ALU.mult, ALU.min).then_inc(f_step, 1)
            dve.wait_ge(f_act, 2)
            v.scalar_tensor_tensor(log_f[:, :, :], fz[:, :, :], 0.0, fe[:, :, :], ALU.min, ALU.subtract).then_inc(f_step, 1)
            dve.wait_ge(f_act, 3)
            v.scalar_tensor_tensor(nf_lo[:, :], ps[0:H, NB + 1, 0:T], -1.0, nf_hi[:, :].bitcast(F32), ALU.mult, ALU.subtract).then_inc(f_rows, 1)
            v.tensor_copy(f_tok[:, :, :], ps[:, NB + 2, 0:TT * H].rearrange("p (a h) -> p a h", a=TT)).then_inc(f_rows, 1)
            dve.wait_ge(f_rows, 2)

            def attend(g, par):
                s_bank, t_bank = NB * par, NB * (1 - par)
                f_g = f_tok[:, :, ds(NB * g, NB)]
                dve.wait_ge(scores_done, g + 1)
                for b in range(TT):
                    v.tensor_reduce(row_max[:, b, :], ps[:, s_bank:s_bank + NB, P * b:P * b + P * (b + 1)], AX.X,
                                    ALU.max).then_inc(max_step, 1)
                dve.wait_ge(max_step, 4 * g + 2)
                v.tensor_tensor(row_max[:, :, :], row_max[:, :, :], f_g, ALU.add).then_inc(max_step, 1)
                dve.wait_ge(max_step, 4 * g + 3)
                v.tensor_tensor(exp_bias[:, :, :], f_g, row_max[:, :, :], ALU.subtract).then_inc(max_step, 1)
                dve.wait_ge(exp_done, 8 * g + 8)
                v.reciprocal(row_inv[:, :, :], row_sum[:, :, :]).then_inc(norm_p, 1)
                dve.wait_ge(norm_p, 3 * g + 1)
                for b, pr in enumerate((prob0, prob1)):
                    n = P * (b + 1)
                    v.tensor_tensor(pr, pr, row_inv[:, b, :].rearrange("p (j o) -> p j o", o=1).broadcast_to([P, NB, n]),
                                    ALU.mult).then_inc(norm_p, 1)
                dve.wait_ge(pt_hi_ready, g + 1)
                v.tensor_tensor(pt_lo, ps[:, t_bank:t_bank + NB, 0:T + P], pt_hi.bitcast(F32), ALU.subtract).then_inc(pt_ready, 1)
                dve.wait_ge(attn_hi, g + 1)
                v.tensor_tensor(mid[:, ds(NB * g, NB), 1, :], ps[:, s_bank:s_bank + NB, 0:T],
                                mid[:, ds(NB * g, NB), 0, :].bitcast(F32), ALU.subtract).then_inc(attn_ready, 1)

            with dve.Fori(0, NG // 2) as r:
                for i in range(2):
                    g = 2 * r + i
                    for t in range(3):
                        pos = 3 * i + t
                        u = 6 * r + pos

                        def evac():
                            if t == 2:
                                dve.wait_ge(qkv_hi, 3 * g + 3)
                                v.tensor_tensor(vs[:, :, 1, :], ps[:, NB * (pos % 2):NB * (pos % 2) + TT, :],
                                                vs[:, :, 0, :].bitcast(F32), ALU.subtract).then_inc(evacuated, 1)
                            else:
                                dst = (qs, ks)[t]
                                whole(u, pos % 2, fsum, SCALE if t == 0 else 1.0, n_half=2 * g + t + 1,
                                      used=((qkv_ready, 2 * g + t),))
                                dve.wait_ge(qkv_hi, 3 * g + t + 1)
                                v.tensor_tensor(dst[:, :, 1, :], fsum, dst[:, :, 0, :].bitcast(F32), ALU.subtract).then_inc(qkv_ready, 1)
                        body(u, evac, (u + A_START, pos % 2), (u + A_START - 1, NB * ((pos + 1) % 2)))
                    attend(g, (3 * i + 3) % 2)
            HALVES0 = U_OUT0 - NG
            with dve.Fori(0, NG // 2) as r:
                for i in range(2):
                    n = 2 * r + i
                    u = U_OUT0 + n
                    body(u, lambda: residual(u, i, NB * n, u - NG + 1, n),
                         (u + A_START, i), (u + A_START - 1, NB * ((i + 1) % 2)))
            ada_store(A_MLP0 - 1, 0)

            def mlp_slice(s, base, l, adas, last=False):
                n_hid = SLICES * NG * l + NG * s
                n_add = NG * (1 + l) + n_hid
                for n in range(NG):
                    u = base + 2 * NG * s + n
                    a = A_MLP0 + NG * s + n // 2

                    def evac():
                        whole(u, n % 2, fsum, n_half=u - NG + 1,
                              used=((hid_ready, n_hid + n), (added, n_add)))
                        dve.wait_ge(evacuated, u + 3)
                        v.scalar_tensor_tensor(fsum, fsum, 0.0, fsum, ALU.max, ALU.mult).then_inc(relu2, 1)
                        dve.wait_ge(hid_hi, SLICES * NG * l + NG * s + n + 1)
                        v.tensor_tensor(mid[:, NB * n:NB * (n + 1), 1, :], fsum,
                                        mid[:, NB * n:NB * (n + 1), 0, :].bitcast(F32), ALU.subtract).then_inc(hid_ready, 1)
                    body(u, evac, (a, (n // 2) % 2) if adas and n % 2 == 0 else None,
                         (a, NB * ((n + 1) % 2)) if adas and n % 2 else None)
                for n in range(NG):
                    u = base + 2 * NG * s + NG + n
                    a = A_MLP0 + NG * s + NG // 2 + n // 2
                    body(u, lambda: residual(u, n % 2, NB * n, u - NG + 1, n_add + n, ((hid_ready, n_hid + NG),)),
                         (a, (n // 2) % 2) if adas and n % 2 == 0 else None,
                         (a, NB * ((n + 1) % 2)) if adas and n % 2 else None, more=not (last and n == NG - 1))

            norm(1, MLP_GAIN[0], 4 * KC, A_MLP0 + 1)
            dve.wait_ge(h_ready, 2 * NQ)
            with dve.Fori(0, SLICES) as s:
                mlp_slice(s, U_MLP0, 0, True)
            norm(2, MIX_GAIN[1], NROW + KC, A_CONV + 1)
            v.memset(conv_u[:, :, 0:2], 0.0).then_inc(conv_zero, 1)
            dve.wait_ge(conv_zero, 1)
            dve.wait_ge(h_ready, 3 * NQ)
            with dve.Fori(0, NG // 2) as r:
                for i in range(2):
                    g = 2 * r + i
                    for t in range(3):
                        pos = 3 * i + t
                        u = U_CONV + 6 * r + pos
                        a = A_CONV + 4 * r + 2 * i + t

                        def evac():
                            whole(u, pos % 2, (conv_b[:, :, :], conv_c[:, :, :], fsum)[t], n_half=u - NG + 1)
                            if t == 2:
                                dve.wait_ge(evacuated, u + 3)
                                v.tensor_tensor(conv_u[:, :, 2:T + 2], conv_c[:, :, :], fsum, ALU.mult).then_inc(conv_in, 1)
                                dve.wait_ge(conv_in, g + 1)
                                dve.wait_ge(conv_tap, g + 1)
                                for tap in (1, 2):
                                    for j in range(NB):
                                        v.scalar_tensor_tensor(
                                            conv_y[:, j, :], conv_u[:, j, tap:tap + T], taps[:, ds(KC * tap + NB * g + j, 1)],
                                            conv_y[:, j, :], ALU.mult, ALU.add).then_inc(conv_step, 1)
                                    dve.wait_ge(conv_step, 2 * NB * g + NB * tap)
                                v.tensor_tensor(conv_y[:, :, :], conv_b[:, :, :], conv_y[:, :, :], ALU.mult).then_inc(conv_gated, 1)
                                dve.wait_ge(conv_hi, g + 1)
                                v.tensor_tensor(mid[:, ds(NB * g, NB), 1, :], conv_y[:, :, :],
                                                mid[:, ds(NB * g, NB), 0, :].bitcast(F32), ALU.subtract).then_inc(conv_ready, 1)
                        body(u, evac, (a, t % 2) if t < 2 else None, (a - 1, NB * ((pos + 1) % 2)) if t else None)
            with dve.Fori(0, NG // 2) as r:
                for i in range(2):
                    n = 2 * r + i
                    u = U_OUT1 + n
                    body(u, lambda: residual(u, i, NB * n, u - NG + 1, NG * (1 + SLICES) + n))
            norm(3, MLP_GAIN[1], NROW + 4 * KC, A_END + 1)
            dve.wait_ge(h_ready, 4 * NQ)
            with dve.Fori(0, SLICES - 1) as s:
                mlp_slice(s, U_MLP1, 1, False)
            mlp_slice(SLICES - 1, U_MLP1, 1, False, last=True)
            norm(4)
            for m in range(NG):
                dve.wait_ge(out_turned, m + 1)
                v.tensor_copy(raw[:, m, 1, :], ps[:, NB + 2 * (m % 2) + 1, :]).then_inc(out_copied1, 1)


_INS = ['x', 'c', 'ada_w', 'ada_b', 'norm_mix', 'norm_mlp', 'fox_w_in', 'fox_b_f', 'fox_w_out', 'conv_w_in',
        'conv_w', 'conv_w_out', 'mlp_w_up', 'mlp_w_down', 'final_norm']


def kernel(**inputs):
    import numpy as _np
    import concourse.bacc as _bacc
    from concourse import mybir as _mybir
    from concourse.bass_utils import run_bass_kernel_spmd as _run

    nc = _bacc.Bacc("TRN2", target_bir_lowering=False, num_devices=1)
    arrays, args = {}, []
    for name in _INS:
        a = _np.ascontiguousarray(inputs[name])
        arrays[f"in_{name}_dram"] = a
        args.append(nc.dram_tensor(f"in_{name}_dram", a.shape, _mybir.dt.from_np(a.dtype), kind="ExternalInput").ap())
    args.append(nc.dram_tensor("out_dram", (1, T, D), F32, kind="ExternalOutput").ap())
    build(nc, *args)
    r = _run(nc, [arrays], core_ids=[0])
    return r.results[0]["out_dram"]
```

```python
from contextlib import ExitStack

import concourse.bass as bass
from concourse import mybir

F32 = mybir.dt.float32
F32R = mybir.dt.float32r
ACT = mybir.ActivationFunctionType
ALU = mybir.AluOpType
AX = mybir.AxisListType

P = 128
D = 2048
T = 256
H = 16
DH = D // H
FF = 4 * D
NMOD = 6
EPS = 1e-6
SCALE = float(DH) ** -0.5
MASKED = -1.0e30

KC = D // P
TT = T // P
NU = 512
NB = NU // P
NG = D // NU
QK = 4
NQ = KC // QK
EK = 2
NE = KC // EK
WR = 4
SLICES = FF // D
NROW = NMOD * KC
VROWS = 96

U_QKV = 0
U_OUT0 = U_QKV + 3 * NG
U_MLP0 = U_OUT0 + NG
U_CONV = U_MLP0 + 2 * NG * SLICES
U_OUT1 = U_CONV + 3 * NG
U_MLP1 = U_OUT1 + NG
A_START = 2 * NG
A_MLP0 = A_START + U_MLP0
A_CONV = A_MLP0 + NG * SLICES
A_END = 2 * NMOD * NG
RING = 2 * NQ
ROUNDS = A_START // 4
A_VE = [0, 1, 3]
A_PE = 2
A_TE = ROUNDS


def build(nc, x, c, ada_w, ada_b, norm_mix, norm_mlp, fox_w_in, fox_b_f, fox_w_out,
          conv_w_in, conv_w, conv_w_out, mlp_w_up, mlp_w_down, final_norm, out):
    ctx = ExitStack()
    with ctx:
        def sb(name, shape, dt=F32):
            return ctx.enter_context(nc.sbuf_tensor(name, shape, dt))

        def sem(name):
            return ctx.enter_context(nc.semaphore(name))

        with nc.sbuf_tensor("start_ring", [P, RING, QK, NU], F32) as start_ring:
            pass
        h = sb("h", [P, KC, 2, T], F32R)
        mid = sb("mid", [P, KC, 2, T], F32R)
        with ExitStack() as shared:
            def early(name, shape, dt=F32):
                return shared.enter_context(nc.sbuf_tensor(name, shape, dt))

            xrow = early("xrow", [P, TT, D])
            vrow = early("vrow", [VROWS, 4, P])
            upto = early("upto", [P, TT, T])
            wf = early("wf", [P, KC, H])
            wf_hi = early("wf_hi", [P, KC, H], F32R)
            wf_lo = early("wf_lo", [P, KC, H], F32R)
        with ExitStack() as shared:
            var = early("var", [P, T])
            inv = early("inv", [P, T])
            newton = early("newton", [P, T])
            squares = early("squares", [P, NQ, T])
        with ExitStack() as shared:
            conv_b = shared.enter_context(nc.sbuf_tensor("conv_b", [P, NB, T], F32))
            conv_c = shared.enter_context(nc.sbuf_tensor("conv_c", [P, NB, T], F32))
            conv_u = shared.enter_context(nc.sbuf_tensor("conv_u", [P, NB, T + 2], F32))
            conv_y = shared.enter_context(nc.sbuf_tensor("conv_y", [P, NB, T], F32))
        qs = sb("qs", [P, NB, 2, T], F32R)
        ks = sb("ks", [P, NB, 2, T], F32R)
        vs = sb("vs", [P, TT, 2, NU], F32R)
        pt_hi = qs[:, :, :, :].rearrange("p j s t -> p (j s t)")[:, 0:NB * 384].rearrange("p (j t) -> p j t", j=NB)
        pt_lo = ks[:, :, :, :].rearrange("p j s t -> p (j s t)")[:, 0:NB * 384].rearrange("p (j t) -> p j t", j=NB)

        xT = sb("xT", [P, KC, T])
        raw = sb("raw", [P, NQ, QK, NU])
        ada_raw = sb("ada_raw", [P, 2, QK, NU])
        w_hi = sb("w_hi", [P, WR, EK, NU], F32R)
        w_lo = sb("w_lo", [P, WR, EK, NU], F32R)
        acc = sb("acc", [P, 2, NU])
        scratch = sb("scratch", [P, 2, NB * T])
        tmp = scratch[:, 0, :].rearrange("p (j t) -> p j t", j=NB)
        fsum = scratch[:, 1, :].rearrange("p (j t) -> p j t", j=NB)
        flat = scratch[:, :, :].rearrange("p s n -> p (s n)")
        prob0 = flat[:, 0:NB * P].rearrange("p (j t) -> p j t", j=NB)
        prob1 = flat[:, NB * P:NB * P * 3].rearrange("p (j t) -> p j t", j=NB)

        ident = sb("ident", [P, P])
        ident_r = sb("ident_r", [P, P], F32R)
        causal = sb("causal", [P, P], F32R)
        ones = sb("ones", [P, P])
        ones_r = sb("ones_r", [P, P], F32R)
        vcol = sb("vcol", [P, 4, VROWS])
        ca = sb("ca", [P, KC])
        ce = sb("ce", [P, 2, KC])
        mod = sb("mod", [P, 2 * NROW])
        gain = sb("gain", [P, KC])
        bf = sb("bf", [P, H])
        fz = sb("fz", [P, TT, H])
        fe = sb("fe", [P, TT, H])
        log_f = sb("log_f", [P, TT, H])
        f_tok = sb("f_tok", [P, TT, H])
        nf_hi = sb("nf_hi", [H, T], F32R)
        nf_lo = sb("nf_lo", [H, T], F32R)
        nf_row = sb("nf_row", [P, NB, T], F32R)
        row_max = sb("row_max", [P, TT, NB])
        exp_bias = sb("exp_bias", [P, TT, NB])
        row_sum = sb("row_sum", [P, TT, NB])
        row_inv = sb("row_inv", [P, TT, NB])

        nf_dram = nc.dram_tensor("nf_dram", (2, H, T), F32, kind="Internal").ap()

        ps = ctx.enter_context(nc.psum_tensor("ps", [P, 8, NU], F32))

        C_COL = vcol[:, 0, 0:KC]
        MIX_GAIN = [vcol[:, 0, KC * (1 + l):KC * (2 + l)] for l in range(2)]
        MLP_GAIN = [vcol[:, 0, KC * (3 + l):KC * (4 + l)] for l in range(2)]
        FINAL = vcol[:, 0, KC * 5:KC * 6]
        ada_bias = vcol[:, 1:3, :].rearrange("p a n -> p (a n)")
        taps = vcol[:, 3, 0:3 * KC]

        x_arrived = sem("x_arrived")
        vec_arrived = sem("vec_arrived")
        wf_arrived = sem("wf_arrived")
        start_arrived = [sem(f"start_arrived{i}") for i in range(RING)]
        raw_arrived = [sem(f"raw_arrived{i}") for i in range(NQ)]
        ada_arrived = [sem(f"ada_arrived{i}") for i in range(2)]
        start_used = sem("start_used")
        nf_arrived = sem("nf_arrived")
        nf_stored = sem("nf_stored")
        out_written = sem("out_written")
        const_ready = sem("const_ready")
        vec_turned = sem("vec_turned")
        vec_ready = sem("vec_ready")
        c_exp = sem("c_exp")
        c_step = sem("c_step")
        x_turned = sem("x_turned")
        hi_ready = sem("hi_ready")
        split_ready = sem("split_ready")
        split_used = sem("split_used")
        half_ready = sem("half_ready")
        evacuated = sem("evacuated")
        ada_steps = sem("ada_steps")
        ada_summed = sem("ada_summed")
        mod_ready = sem("mod_ready")
        squared = sem("squared")
        var_ready = sem("var_ready")
        conv_zero = sem("conv_zero")
        reduced = sem("reduced")
        normed = sem("normed")
        gain_ready = sem("gain_ready")
        norm_step = sem("norm_step")
        root_ready = sem("root_ready")
        scaled = sem("scaled")
        modulated = sem("modulated")
        h_hi = sem("h_hi")
        h_ready = sem("h_ready")
        f_split = sem("f_split")
        f_lo = sem("f_lo")
        f_done = sem("f_done")
        f_step = sem("f_step")
        f_act = sem("f_act")
        f_rows = sem("f_rows")
        qkv_hi = sem("qkv_hi")
        qkv_ready = sem("qkv_ready")
        scores_done = sem("scores_done")
        max_step = sem("max_step")
        exp_done = sem("exp_done")
        norm_p = sem("norm_p")
        turned = sem("turned")
        pt_hi_ready = sem("pt_hi_ready")
        pt_ready = sem("pt_ready")
        pv_done = sem("pv_done")
        attn_hi = sem("attn_hi")
        attn_ready = sem("attn_ready")
        gated = sem("gated")
        added = sem("added")
        relu2 = sem("relu2")
        hid_hi = sem("hid_hi")
        hid_ready = sem("hid_ready")
        conv_in = sem("conv_in")
        conv_tap = sem("conv_tap")
        conv_step = sem("conv_step")
        conv_gated = sem("conv_gated")
        conv_hi = sem("conv_hi")
        conv_ready = sem("conv_ready")
        out_turned = sem("out_turned")
        out_copied0 = sem("out_copied0")
        out_copied1 = sem("out_copied1")

        block = ctx.enter_context(nc.Block())

        def pair(e):
            return scratch[:, (e // 2) % 2, NU * (e % 2):NU * (e % 2 + 1)].rearrange("p (k t) -> p k t", k=EK)

        def ds(start, size):
            return bass.ds(start, size)

        def quarter(w, row0, q, col, width=NU):
            return w.rearrange("(k p) n -> p k n", p=P)[:, ds(row0 + QK * q, QK), ds(col, width)]

        def ada_quarter(a_layer, n, q):
            return quarter(ada_w[a_layer], 0, q, NU * n)

        @block.sync
        def _(sp):
            sp.dma_start(vrow[0:KC, 0, :], c.rearrange("b (k p) -> (b k) p", p=P)).then_inc(vec_arrived, 16)
            sp.dma_start(vrow[KC:3 * KC, 0, :], norm_mix.rearrange("l (k p) -> (l k) p", p=P)).then_inc(vec_arrived, 16)
            sp.dma_start(vrow[3 * KC:5 * KC, 0, :], norm_mlp.rearrange("l (k p) -> (l k) p", p=P)).then_inc(vec_arrived, 16)
            sp.dma_start(vrow[5 * KC:6 * KC, 0, :], final_norm.rearrange("(k p) -> k p", p=P)).then_inc(vec_arrived, 16)
            for l in range(2):
                sp.dma_start(vrow[:, 1 + l, :], ada_b[l].rearrange("(k p) -> k p", p=P)).then_inc(vec_arrived, 16)
            sp.dma_start(vrow[0:3 * KC, 3, :], conv_w[0].rearrange("a (k p) -> (a k) p", p=P)).then_inc(vec_arrived, 16)
            sp.dma_start(xrow[:, :, :], x[0].rearrange("(a p) n -> p a n", p=P)).then_inc(x_arrived, 16)
            sp.dma_start(wf[:, :, :], fox_w_in[0].rearrange("(k p) n -> p k n", p=P)[:, :, 3 * D:3 * D + H]).then_inc(wf_arrived, 16)
            sp.dma_start(bf[:, :], fox_b_f.broadcast_to([P, H])).then_inc(wf_arrived, 16)

            def unit(u, w, row0, col):
                for q in range(NQ):
                    sp.wait_ge(split_ready, NE * u + 2 * q + 2)
                    sp.dma_start(raw[:, q], quarter(w, row0, q, col)).then_inc(raw_arrived[q], 16)

            def mlp(l, base):
                with sp.Fori(0, SLICES) as s:
                    for n in range(NG):
                        unit(base + 2 * NG * s + n, mlp_w_up[l], 0, D * s + NU * n)
                    for n in range(NG):
                        unit(base + 2 * NG * s + NG + n, mlp_w_down[l], KC * s, NU * n)

            sp.wait_ge(start_used, NQ * ROUNDS)
            with sp.Fori(0, NG) as g:
                for part in range(3):
                    unit(U_QKV + 3 * g + part, fox_w_in[0], 0, D * part + NU * g)
            with sp.Fori(0, NG) as n:
                unit(U_OUT0 + n, fox_w_out[0], 0, NU * n)
            mlp(0, U_MLP0)
            with sp.Fori(0, NG) as g:
                for part in range(3):
                    unit(U_CONV + 3 * g + part, conv_w_in[0], 0, D * part + NU * g)
            with sp.Fori(0, NG) as n:
                unit(U_OUT1 + n, conv_w_out[0], 0, NU * n)
            mlp(1, U_MLP1)
            for m in range(NG):
                sp.wait_ge(out_copied0, m + 1)
                sp.wait_ge(out_copied1, m + 1)
                sp.dma_start(out[0].rearrange("(a p) n -> p a n", p=P)[:, :, NU * m:NU * (m + 1)],
                             raw[:, m, 0:TT, :]).then_inc(out_written, 16)
            sp.wait_ge(out_written, 16 * NG)

        @block.gpsimd
        def _(pool):
            def start_load(r, q, ve):
                unit = 4 * r + (A_VE[q // NQ] if ve else A_PE)
                slot = q % NQ + (0 if ve else NQ)
                if ve and (r or q >= NQ):
                    pool.wait_ge(ada_steps, QK * (3 * NQ * r + q - NQ + 1))
                elif not ve and r:
                    pool.wait_ge(start_used, NQ * (r - 1) + q + 1)
                pool.dma_start(start_ring[:, slot], ada_quarter(0, unit, q % NQ)).then_inc(start_arrived[slot], 16)

            def start_round(r, part):
                for p in part:
                    start_load(r, p, False)
                    for q in range(3 * p, 3 * p + 3):
                        start_load(r, q, True)

            start_round(0, range(0, 1))
            pool.memset(ident[:, :], 0.0).then_inc(const_ready, 1)
            pool.memset(ident_r[:, :].bitcast(F32), 0.0).then_inc(const_ready, 1)
            pool.memset(causal[:, :].bitcast(F32), 0.0).then_inc(const_ready, 1)
            pool.memset(upto[:, :, :], 1.0).then_inc(const_ready, 1)
            pool.memset(ones[:, :], 1.0).then_inc(const_ready, 1)
            pool.memset(ones_r[:, :].bitcast(F32), 1.0).then_inc(const_ready, 1)
            pool.memset(nf_row[:, :, :].bitcast(F32), 0.0).then_inc(const_ready, 1)
            pool.wait_ge(const_ready, 7)
            for m in (ident, ident_r):
                pool.affine_select(out=m[:, :], in_=m[:, :].bitcast(F32), compare_op=ALU.not_equal, fill=1.0,
                                   base=0, pattern=[[-1, P]], channel_multiplier=1).then_inc(const_ready, 1)
            pool.affine_select(out=causal[:, :], in_=causal[:, :].bitcast(F32), compare_op=ALU.is_ge, fill=MASKED,
                               base=0, pattern=[[-1, P]], channel_multiplier=1).then_inc(const_ready, 1)
            for a in range(TT):
                pool.affine_select(out=upto[:, a, :], in_=upto[:, a, :], compare_op=ALU.is_ge, fill=0.0,
                                   base=-P * a, pattern=[[1, T]], channel_multiplier=-1).then_inc(const_ready, 1)
            start_round(0, range(1, NQ))
            for r in range(1, ROUNDS):
                start_round(r, range(NQ))

            def ada_units(layer, first, a0, a1):
                with pool.Fori(a0, a1) as a:
                    for q in range(NQ):
                        if first is None or q >= 2:
                            pool.wait_ge(ada_steps, KC * (a - A_TE) + QK * (q - 1))
                        pool.dma_start(ada_raw[:, q % 2], ada_quarter(layer, a - NMOD * NG * layer, q)
                                       ).then_inc(ada_arrived[q % 2], 16)

            ada_units(0, 1, A_START, A_START + 1)
            ada_units(0, None, A_START + 1, NMOD * NG)
            ada_units(1, None, NMOD * NG, A_END)

        @block.tensor
        def _(pe):
            mm = nc.tensor.matmul

            def multiply(u, par, rhs, ada=None, tokens_out=False, ready=None, after=None):
                pe.wait_ge(evacuated, u + 1)
                for e in range(NE):
                    pe.wait_ge(split_ready, NE * u + e + NE + 1)
                    if ready is not None:
                        ready(e)
                    for kk in range(EK):
                        k = EK * e + kk
                        hi, lo = w_hi[:, e % WR, kk, :], w_lo[:, e % WR, kk, :]
                        if tokens_out:
                            for a in range(TT):
                                o = ps[:, NB * par + a, :]
                                xh, xl = rhs[:, k, 0, P * a:P * (a + 1)], rhs[:, k, 1, P * a:P * (a + 1)]
                                mm(o, xh, hi, start=(k == 0), stop=False)
                                mm(o, xl, hi, start=False, stop=False)
                                last = mm(o, xh, lo, start=False, stop=(k == KC - 1))
                        else:
                            for j in range(NB):
                                cols = slice(P * j, P * (j + 1))
                                mm(ps[:, NB * par + j, :], hi[:, cols], rhs[:, k, :, :].rearrange("p s t -> p (s t)"),
                                   start=(k == 0), stop=False)
                                last = mm(ps[:, NB * par + j, 0:T], lo[:, cols], rhs[:, k, 0, :],
                                          start=False, stop=(k == KC - 1))
                    last.then_inc(split_used, 1)
                    if e == NE // 2 - 1 and ada is not None:
                        pe.wait_ge(evacuated, u + 2)
                        ada_sum(*ada, NB * par + NB - 1 if tokens_out else NB * (1 - par))
                    if after is not None and e in after:
                        after[e]()

            def ada_sum(a, slot, bank):
                pe.wait_ge(ada_steps, KC * (a - A_TE + 1))
                for j in range(NB):
                    last = mm(ps[:, bank, j:j + 1], acc[:, slot, P * j:P * (j + 1)], ones[:, 0:1],
                              start=True, stop=True)
                last.then_inc(ada_summed, 1)

            def norm_sum(i):
                for m in range(NQ):
                    pe.wait_ge(reduced, (NQ, 2 * NQ, NQ * (2 + SLICES), NQ * (3 + SLICES),
                                         NQ * (3 + 2 * SLICES))[i] - NQ + m + 1)
                    last = mm(ps[:, 0, 0:T], ones[:, :], squares[:, m, :], start=(m == 0), stop=(m == NQ - 1))
                    last.then_inc(normed, 1)

            pe.wait_ge(const_ready, 12)
            pe.wait_ge(vec_arrived, 16 * 7)
            for i in range(4):
                rows = 3 * KC if i == 3 else VROWS
                last = nc.tensor.transpose(ps[:, 7, VROWS * i:VROWS * i + rows], vrow[0:rows, i, :], ident[0:rows, 0:rows])
            last.then_inc(vec_turned, 1)
            pe.wait_ge(x_arrived, 16)
            for half in range(2):
                if half == 1:
                    pe.wait_ge(vec_ready, 1)
                for k in range(8):
                    for a in range(TT):
                        last = nc.tensor.transpose(
                            ps[:, NB * half + k // 2, T * (k % 2) + P * a:T * (k % 2) + P * (a + 1)],
                            xrow[:, a, P * (8 * half + k):P * (8 * half + k + 1)], ident[:, :])
                last.then_inc(x_turned, 1)
            pe.wait_ge(evacuated, 2)
            norm_sum(0)

            def start_sum(r, i):
                pe.wait_ge(ada_steps, KC * (3 * r + i + 1))
                if r:
                    pe.wait_ge(mod_ready, 4 * (r - 1) + A_VE[i] + 1)
                for j in range(NB):
                    last = mm(ps[:, 1 + i, j:j + 1], acc[:, (3 * r + i) % 2, P * j:P * (j + 1)], ones[:, 0:1],
                              start=True, stop=True)
                last.then_inc(ada_summed, 2 if i == 2 else 1)

            pe.wait_ge(c_step, 4)
            for r in range(ROUNDS):
                if r:
                    pe.wait_ge(mod_ready, 4 * (r - 1) + A_PE + 1)
                for q in range(NQ):
                    pe.wait_ge(start_arrived[NQ + q], 16 * r + 16)
                    for k in range(QK * q, QK * (q + 1)):
                        for j in range(NB):
                            last = mm(ps[:, NB + j, 0:1], start_ring[:, NQ + q, k % QK, P * j:P * (j + 1)],
                                      ca[:, k:k + 1], start=(k == 0), stop=(k == KC - 1))
                    last.then_inc(start_used, 1)
                    if q > 0:
                        start_sum(r, q - 1)

            def h_chunks(i):
                return lambda e: pe.wait_ge(h_ready, NE * i + e + 1)

            def mid_chunks(sem, n):
                return lambda e: e % 2 or pe.wait_ge(sem, n + e // 2 + 1)

            pe.wait_ge(f_lo, 1)
            for k in range(KC):
                if k % EK == 0:
                    pe.wait_ge(h_ready, k // EK + 1)
                for a in range(TT):
                    o = ps[:, NB + 1 + a, 0:H]
                    xh, xl = h[:, k, 0, P * a:P * (a + 1)], h[:, k, 1, P * a:P * (a + 1)]
                    mm(o, xh, wf_hi[:, k, :], start=(k == 0), stop=False)
                    mm(o, xl, wf_hi[:, k, :], start=False, stop=False)
                    last = mm(o, xh, wf_lo[:, k, :], start=False, stop=(k == KC - 1))
            last.then_inc(f_done, 1)

            def forget_sums():
                pe.wait_ge(f_step, 3)
                pe.wait_ge(evacuated, 3)
                for a in range(TT):
                    mm(ps[0:H, 1, 0:T], log_f[:, a, :], upto[:, a, :], start=(a == 0), stop=(a == TT - 1))
                for b in range(TT):
                    for a in range(TT):
                        last = mm(ps[:, 2, H * b:H * (b + 1)], upto[:, a, P * b:P * (b + 1)], log_f[:, a, :],
                                  start=(a == 0), stop=(a == TT - 1))
                last.then_inc(f_done, 1)

            def scores(g, s_bank):
                pe.wait_ge(qkv_ready, 2 * g + 2)
                pe.wait_ge(nf_arrived, 16 * g + 16)
                for j in range(NB):
                    for b in range(TT):
                        n = P * (b + 1)
                        o = ps[:, s_bank + j, P * b:P * b + n]
                        qh, ql = qs[:, j, 0, P * b:P * (b + 1)], qs[:, j, 1, P * b:P * (b + 1)]
                        mm(o, qh, ks[:, j, 0, 0:n], start=True, stop=False)
                        mm(o, qh, ks[:, j, 1, 0:n], start=False, stop=False)
                        mm(o, ql, ks[:, j, 0, 0:n], start=False, stop=False)
                        mm(o, ones_r[:, :], nf_row[:, j, 0:n], start=False, stop=False)
                        last = mm(o[:, n - P:n], ident_r[:, :], causal[:, :], start=False, stop=True)
                last.then_inc(scores_done, 1)

            def turn(g, s_bank):
                pe.wait_ge(norm_p, 3 * g + 3)
                for j in range(NB):
                    nc.tensor.transpose(ps[:, s_bank + j, 0:P], prob0[:, j, :], ident[:, :])
                    for b in range(TT):
                        last = nc.tensor.transpose(ps[:, s_bank + j, P * (b + 1):P * (b + 2)],
                                                   prob1[:, j, P * b:P * (b + 1)], ident[:, :])
                last.then_inc(turned, 1)

            def mix_values(g, o_bank):
                pe.wait_ge(pt_ready, g + 1)
                pe.wait_ge(evacuated, 3 * g + 2 + 3)
                for j in range(NB):
                    o = ps[:, o_bank + j // 2, T * (j % 2):T * (j % 2) + T]
                    for b, part, dst in ((0, slice(0, T), o), (1, slice(T, T + P), o[:, P:T])):
                        vh, vl = vs[:, b, 0, P * j:P * (j + 1)], vs[:, b, 1, P * j:P * (j + 1)]
                        mm(dst, vh, pt_hi[:, j, part], start=(b == 0), stop=False)
                        mm(dst, vh, pt_lo[:, j, part], start=False, stop=False)
                        last = mm(dst, vl, pt_hi[:, j, part], start=False, stop=(b == 1))
                last.then_inc(pv_done, 1)

            def mod_read(a):
                pe.wait_ge(mod_ready, a + 1)

            for g in range(NG):
                u = 3 * g
                if g:
                    pe.wait_ge(pt_ready, g)
                multiply(u, u % 2, h, (u + A_START - 1, (u + 1) % 2) if g else None,
                         after={3: lambda: mix_values(g - 1, NB * (1 - u % 2) + 2)} if g else None)
                mod_read(u + A_START - 1)
                u = 3 * g + 1
                if g:
                    pe.wait_ge(attn_ready, g)
                multiply(u, u % 2, h, (u + A_START - 1, (u + 1) % 2), after=None if g else {3: forget_sums})
                mod_read(u + A_START - 1)
                u = 3 * g + 2
                if g == 0:
                    pe.wait_ge(f_rows, 2)
                s_bank = NB * (1 - u % 2)
                multiply(u, u % 2, h, (u + A_START - 1, (u + 1) % 2), tokens_out=True,
                         after={2: lambda: scores(g, s_bank), 6: lambda: turn(g, s_bank)})
                mod_read(u + A_START - 1)
            for n in range(NG):
                u = U_OUT0 + n
                if n == 0:
                    pe.wait_ge(pt_ready, NG)
                if n == 1:
                    pe.wait_ge(attn_ready, NG)
                multiply(u, u % 2, mid, (u + A_START - 1, (u + 1) % 2),
                         ready=None if n else mid_chunks(attn_ready, 0),
                         after=None if n else {3: lambda: mix_values(NG - 1, NB + 2)})
                mod_read(u + A_START - 1)

            def mlp(base, i, adas):
                norm_sum(i)
                with pe.Fori(0, SLICES) as s:
                    for n in range(2 * NG):
                        u = base + 2 * NG * s + n
                        a = A_MLP0 + NG * s + n // 2 - 1
                        ready = {0: h_chunks(i), NG: mid_chunks(hid_ready, (SLICES * (i // 2) + s) * NG)}.get(n)
                        multiply(u, n % 2, h if n < NG else mid, (a, (n // 2 + 1) % 2) if adas and n % 2 == 0 else None,
                                 ready=ready)
                        if adas and n % 2 == 0:
                            mod_read(a)

            mlp(U_MLP0, 1, True)
            ada_sum(A_CONV - 1, 1, 0)
            mod_read(A_CONV - 1)
            norm_sum(2)
            with pe.Fori(0, NG // 2) as r:
                for i in range(2):
                    for t in range(3):
                        pos = 3 * i + t
                        a = A_CONV + 4 * r + 2 * i + t - 1
                        multiply(U_CONV + 6 * r + pos, pos % 2, h, (a, (t + 1) % 2) if t else None,
                                 ready=None if pos else h_chunks(2))
                        if t:
                            mod_read(a)
            with pe.Fori(0, NG // 2) as r:
                for i in range(2):
                    multiply(U_OUT1 + 2 * r + i, i, mid, ready=None if i else mid_chunks(conv_ready, 0))
            mlp(U_MLP1, 3, False)
            norm_sum(4)
            for m in range(NG):
                pe.wait_ge(modulated, NE * (2 * 4) + 4 * (m + 1))
                if m >= 2:
                    pe.wait_ge(out_copied0, m - 1)
                    pe.wait_ge(out_copied1, m - 1)
                for a in range(TT):
                    for j in range(NB):
                        last = nc.tensor.transpose(ps[:, NB + 2 * (m % 2) + a, P * j:P * (j + 1)],
                                                   scratch[:, m % 2, T * j + P * a:T * j + P * (a + 1)], ident[:, :])
                last.then_inc(out_turned, 1)

        @block.scalar
        def _(act):
            op = nc.scalar.activation

            def split(u, e, first=False):
                if e % 2 == 0:
                    act.wait_ge(raw_arrived[e // 2], 16 * u + 16)
                if not first:
                    act.wait_ge(split_used, NE * u + e - WR + 1)
                op(w_hi[:, e % WR], raw[:, e // 2, EK * (e % 2):EK * (e % 2 + 1)], ACT.Copy).then_inc(hi_ready, 1)

            def body(u, evac, more=True, after=None):
                for i, (du, e) in enumerate(((0, 4), (0, 6), (1, 0), (1, 2))):
                    if du == 0 or more:
                        split(u + du, e)
                        split(u + du, e + 1)
                    if after is not None and i in after:
                        after[i]()
                act.wait_ge(split_used, NE * u + NE)
                evac()

            def half(u, par, scale=1.0, n_red=NQ):
                act.wait_ge(evacuated, u + 2)
                act.wait_ge(reduced, n_red)
                op(tmp, ps[:, NB * par:NB * (par + 1), T:2 * T], ACT.Copy, scale=scale).then_inc(half_ready, 1)

            def residual(u, par, gate0, k, n_res):
                half(u, par, n_red=NQ + n_res)
                act.wait_ge(evacuated, u + 3)
                for j in range(NB):
                    last = op(fsum[:, j, :], fsum[:, j, :], ACT.Copy, scale=mod[:, ds(gate0 + k + j, 1)])
                last.then_inc(gated, 1)
                act.wait_ge(added, n_res + 1)
                op(tmp, xT[:, ds(k, NB), :], ACT.Square).then_inc(squared, 1)

            act.wait_ge(vec_ready, 1)
            op(ce[:, 0, :], C_COL, ACT.Exp, scale=-1.0).then_inc(c_exp, 1)
            act.wait_ge(evacuated, 2)
            for m in range(NQ):
                act.wait_ge(reduced, m)
                op(tmp, xT[:, QK * m:QK * (m + 1), :], ACT.Square).then_inc(squared, 1)
            act.wait_ge(norm_step, 1)
            op(inv[:, :], newton[:, :], ACT.Sqrt).then_inc(root_ready, 1)
            act.wait_ge(wf_arrived, 32)
            op(wf_hi[:, :, :], wf[:, :, :], ACT.Copy).then_inc(f_split, 1)

            def root(i):
                act.wait_ge(norm_step, 5 * i + 1)
                op(inv[:, :], newton[:, :], ACT.Sqrt).then_inc(root_ready, 1)

            def norm(i, out_norm=False):
                if i:
                    root(i)
                if out_norm:
                    return
                for e in range(NE):
                    act.wait_ge(modulated, EK * (NE * i + e + 1))
                    op(h[:, EK * e:EK * (e + 1), 0, :], pair(e), ACT.Copy).then_inc(h_hi, 1)

            norm(0)
            for e in range(WR):
                split(0, e, True)
            act.wait_ge(f_step, 2)
            op(fe[:, :, :], fe[:, :, :], ACT.Exp).then_inc(f_act, 1)
            act.wait_ge(f_act, 1)
            op(fe[:, :, :], fe[:, :, :], ACT.Ln, bias=1.0).then_inc(f_act, 1)

            def forget_rows():
                act.wait_ge(f_done, 2)
                op(nf_hi[:, :], ps[0:H, 1, 0:T], ACT.Copy, scale=-1.0).then_inc(f_act, 1)
                act.wait_ge(f_rows, 2)
                act.wait_ge(f_act, 3)
                act.dma_start(nf_dram[0], nf_hi[:, :].bitcast(F32)).then_inc(nf_stored, 16)
                act.dma_start(nf_dram[1], nf_lo[:, :].bitcast(F32)).then_inc(nf_stored, 16)

            def load_nf(g):
                if g == 0:
                    act.wait_ge(nf_stored, 32)
                    act.wait_ge(const_ready, 12)
                act.wait_ge(scores_done, g)
                act.dma_start(nf_row[0:2, :, :].bitcast(F32), nf_dram[:, NB * g:NB * (g + 1), :]).then_inc(nf_arrived, 16)

            def exps(g, s_bank):
                act.wait_ge(max_step, 4 * g + 4)
                for j in range(NB):
                    for b in range(TT):
                        dst = prob0[:, j, :] if b == 0 else prob1[:, j, :]
                        op(dst, ps[:, s_bank + j, P * b:P * b + P * (b + 1)], ACT.Exp, bias=exp_bias[:, b, j:j + 1],
                           accum_out=row_sum[:, b, j:j + 1]).then_inc(exp_done, 1)

            def round_probs(g, s_bank):
                act.wait_ge(turned, g + 1)
                op(pt_hi, ps[:, s_bank:s_bank + NB, 0:T + P], ACT.Copy).then_inc(pt_hi_ready, 1)

            def round_attn(g, o_bank):
                act.wait_ge(pv_done, g + 1)
                op(mid[:, NB * g:NB * (g + 1), 0, :], ps[:, o_bank:o_bank + 2, :].rearrange("p b (j t) -> p (b j) t", j=2),
                   ACT.Copy).then_inc(attn_hi, 1)

            for g in range(NG):
                for t in range(3):
                    u = 3 * g + t
                    par = u % 2

                    def evac():
                        if t == 2:
                            op(vs[:, :, 0, :], ps[:, NB * par:NB * par + TT, :], ACT.Copy).then_inc(qkv_hi, 1)
                        else:
                            half(u, par, SCALE if t == 0 else 1.0)
                            act.wait_ge(evacuated, u + 3)
                            op((qs, ks)[t][:, :, 0, :], fsum, ACT.Copy).then_inc(qkv_hi, 1)
                            if t == 1:
                                load_nf(g)
                    after = None
                    if t == 0 and g:
                        after = {1: lambda: round_attn(g - 1, NB * (1 - par) + 2)}
                    elif t == 1 and g == 0:
                        after = {1: forget_rows}
                    elif t == 2:
                        after = {0: lambda: exps(g, NB * (1 - par)), 2: lambda: round_probs(g, NB * (1 - par))}
                    body(u, evac, after=after)
            for n in range(NG):
                body(U_OUT0 + n, lambda: residual(U_OUT0 + n, n % 2, 2 * KC, NB * n, n),
                     after=None if n else {1: lambda: round_attn(NG - 1, NB + 2)})

            def mlp_slice(s, base, l, last=False):
                for n in range(NG):
                    u = base + 2 * NG * s + n

                    def evac():
                        half(u, n % 2, n_red=NQ + NG * (1 + l) + SLICES * NG * l + NG * s)
                        act.wait_ge(relu2, SLICES * NG * l + NG * s + n + 1)
                        op(mid[:, NB * n:NB * (n + 1), 0, :], fsum, ACT.Copy).then_inc(hid_hi, 1)
                    body(u, evac)
                for n in range(NG):
                    u = base + 2 * NG * s + NG + n
                    body(u, lambda: residual(u, n % 2, NROW * l + 5 * KC, NB * n,
                                             NG * (1 + l) + SLICES * NG * l + NG * s + n), more=not (last and n == NG - 1))

            norm(1)
            with act.Fori(0, SLICES) as s:
                mlp_slice(s, U_MLP0, 0)
            norm(2)
            with act.Fori(0, NG // 2) as r:
                for i in range(2):
                    g = 2 * r + i
                    for t in range(3):
                        pos = 3 * i + t
                        u = U_CONV + 6 * r + pos

                        def evac():
                            half(u, pos % 2, n_red=NQ + NG * (1 + SLICES))
                            if t == 2:
                                act.wait_ge(conv_in, g + 1)
                                act.wait_ge(conv_ready, g)
                                for j in range(NB):
                                    last = op(conv_y[:, j, :], conv_u[:, j, 0:T], ACT.Copy, scale=taps[:, ds(NB * g + j, 1)])
                                last.then_inc(conv_tap, 1)
                                act.wait_ge(conv_gated, g + 1)
                                op(mid[:, ds(NB * g, NB), 0, :], conv_y[:, :, :], ACT.Copy).then_inc(conv_hi, 1)
                        body(u, evac)
            for n in range(NG):
                body(U_OUT1 + n, lambda: residual(U_OUT1 + n, n % 2, NROW + 2 * KC, NB * n, NG * (1 + SLICES) + n))
            norm(3)
            with act.Fori(0, SLICES - 1) as s:
                mlp_slice(s, U_MLP1, 1)
            mlp_slice(SLICES - 1, U_MLP1, 1, last=True)
            norm(4, out_norm=True)
            for m in range(NG):
                act.wait_ge(out_turned, m + 1)
                op(raw[:, m, 0, :], ps[:, NB + 2 * (m % 2), :], ACT.Copy).then_inc(out_copied0, 1)

        @block.vector
        def _(dve):
            v = nc.vector

            def split(u, e):
                dve.wait_ge(hi_ready, NE * u + e + 1)
                v.tensor_tensor(w_lo[:, e % WR], raw[:, e // 2, EK * (e % 2):EK * (e % 2 + 1)],
                                w_hi[:, e % WR].bitcast(F32), ALU.subtract).then_inc(split_ready, 1)

            def ada_add(steps, slot, q, src):
                for kk in range(QK):
                    k = QK * q + kk
                    if k == 0:
                        v.tensor_scalar(acc[:, slot, :], src[:, kk, :], ca[:, 0:1], None, ALU.mult).then_inc(ada_steps, 1)
                    else:
                        dve.wait_ge(ada_steps, steps + k)
                        v.scalar_tensor_tensor(acc[:, slot, :], src[:, kk, :], ca[:, k:k + 1], acc[:, slot, :],
                                               ALU.mult, ALU.add).then_inc(ada_steps, 1)

            def ada_store(a, bank):
                dve.wait_ge(ada_summed, a + 1)
                v.tensor_tensor(mod[:, ds(NB * a, NB)], ps[:, bank, 0:NB], ada_bias[:, ds(NB * a, NB)],
                                ALU.add).then_inc(mod_ready, 1)

            def body(u, evac, ada=None, store=None, more=True, after=None, ada_q=(0, 1, 2, 3), ada_first=False,
                     ada_late=NQ):
                def ada_quarter_of(i):
                    a, slot = ada
                    q = ada_q[i]
                    if q == 0:
                        dve.wait_ge(ada_summed, a - 1)
                    dve.wait_ge(ada_arrived[q % 2], 16 * (2 * (a - A_START) + q // 2 + 1))
                    ada_add(KC * (a - A_TE), slot, q, ada_raw[:, q % 2])

                for i, (du, e) in enumerate(((0, 4), (0, 6), (1, 0), (1, 2))):
                    if du == 0 or more:
                        split(u + du, e)
                        split(u + du, e + 1)
                    if after is not None and i in after and not (ada_first and i == 0):
                        after[i]()
                    if i == 1 and store is not None:
                        ada_store(*store)
                    if ada is not None and ada_q[i] is not None and i < ada_late:
                        ada_quarter_of(i)
                    if ada_first and i == 0:
                        after[i]()
                evac()
                for i in range(ada_late, NQ):
                    ada_quarter_of(i)

            def whole(u, par, dst, scale=1.0, n_half=None, used=()):
                for wait in used:
                    dve.wait_ge(*wait)
                dve.wait_ge(half_ready, n_half)
                if scale == 1.0:
                    v.tensor_tensor(dst, ps[:, NB * par:NB * (par + 1), 0:T], tmp, ALU.add).then_inc(evacuated, 1)
                else:
                    v.scalar_tensor_tensor(dst, ps[:, NB * par:NB * (par + 1), 0:T], scale, tmp,
                                           ALU.mult, ALU.add).then_inc(evacuated, 1)

            def residual(u, par, k, slot, n_half, n_res, used=()):
                whole(u, par, fsum, n_half=n_half, used=((added, n_res),) + used)
                dve.wait_ge(gated, n_res + 1)
                v.tensor_tensor(xT[:, ds(k, NB), :], xT[:, ds(k, NB), :], fsum, ALU.add).then_inc(added, 1)
                dve.wait_ge(squared, NQ + n_res + 1)
                reduce_squares(slot)

            def reduce_squares(m):
                v.tensor_reduce(squares[:, m, :], tmp.rearrange("p k t -> p t k"), AX.X, ALU.add).then_inc(reduced, 1)

            def inverse_rms(i):
                dve.wait_ge(normed, NQ * i + NQ)
                v.tensor_scalar(var[:, :], ps[:, 0, 0:T], 1.0 / D, EPS, ALU.mult, ALU.add).then_inc(var_ready, 1)
                dve.wait_ge(var_ready, i + 1)
                v.reciprocal(newton[:, :], var[:, :]).then_inc(norm_step, 1)
                dve.wait_ge(root_ready, i + 1)
                v.tensor_tensor(newton[:, :], inv[:, :], inv[:, :], ALU.mult).then_inc(norm_step, 1)
                dve.wait_ge(norm_step, 5 * i + 2)
                v.tensor_tensor(newton[:, :], newton[:, :], var[:, :], ALU.mult).then_inc(norm_step, 1)
                dve.wait_ge(norm_step, 5 * i + 3)
                v.tensor_scalar(newton[:, :], newton[:, :], -0.5, 1.5, ALU.mult, ALU.add).then_inc(norm_step, 1)
                dve.wait_ge(norm_step, 5 * i + 4)
                v.tensor_tensor(inv[:, :], inv[:, :], newton[:, :], ALU.mult).then_inc(norm_step, 1)
                dve.wait_ge(norm_step, 5 * i + 5)

            v.memset(gain[:, :], 0.0).then_inc(split_ready, NE)
            dve.wait_ge(vec_turned, 1)
            v.tensor_copy(vcol[:, 0:3, :], ps[:, 7, 0:3 * VROWS].rearrange("p (a n) -> p a n", a=3)).then_inc(c_step, 1)
            v.tensor_copy(vcol[:, 3, 0:3 * KC], ps[:, 7, 3 * VROWS:3 * VROWS + 3 * KC]).then_inc(vec_ready, 1)
            dve.wait_ge(c_exp, 1)
            dve.wait_ge(c_step, 1)
            v.tensor_scalar(ce[:, 1, :], ce[:, 0, :], 1.0, None, ALU.add).then_inc(c_step, 1)
            dve.wait_ge(c_step, 2)
            v.reciprocal(ce[:, 0, :], ce[:, 1, :]).then_inc(c_step, 1)
            dve.wait_ge(c_step, 3)
            v.tensor_tensor(ca[:, :], C_COL, ce[:, 0, :], ALU.mult).then_inc(c_step, 1)
            dve.wait_ge(c_step, 4)

            def x_copies():
                for half in range(2):
                    dve.wait_ge(x_turned, half + 1)
                    v.tensor_copy(xT[:, 8 * half:8 * (half + 1), :],
                                  ps[:, NB * half:NB * (half + 1), :].rearrange("p b (k t) -> p (b k) t", k=2)
                                  ).then_inc(evacuated, 1)

            def start_add(r, i):
                n = 3 * r + i
                if n >= 2:
                    dve.wait_ge(ada_summed, 4 * ((n - 2) // 3) + A_VE[(n - 2) % 3] + 1)
                for q in range(NQ):
                    dve.wait_ge(start_arrived[q], 16 * n + 16)
                    ada_add(KC * n, n % 2, q, start_ring[:, q])
                    if n == 0 and q == 1:
                        x_copies()

            def start_store(r, i):
                ada_store(4 * r + A_VE[i], 1 + i)

            def start_store_pe(r):
                dve.wait_ge(start_used, NQ * r + NQ)
                a = 4 * r + A_PE
                v.tensor_tensor(mod[:, NB * a:NB * (a + 1)], ps[:, NB:2 * NB, 0], ada_bias[:, NB * a:NB * (a + 1)],
                                ALU.add).then_inc(mod_ready, 1)

            start_add(0, 0)
            for m in range(NQ):
                dve.wait_ge(squared, m + 1)
                reduce_squares(m)
            for r in range(ROUNDS):
                if r:
                    start_add(r, 0)
                    start_store_pe(r - 1)
                    start_store(r - 1, 2)
                start_add(r, 1)
                if r == 0:
                    inverse_rms(0)
                start_store(r, 0)
                start_add(r, 2)
                start_store(r, 1)
            start_store_pe(ROUNDS - 1)
            start_store(ROUNDS - 1, 2)
            dve.wait_ge(f_split, 1)
            v.tensor_tensor(wf_lo[:, :, :], wf[:, :, :], wf_hi[:, :, :].bitcast(F32), ALU.subtract).then_inc(f_lo, 1)

            def norm(i, gains=None, shift0=None, n_mod=None):
                if gains is not None:
                    dve.wait_ge(mod_ready, n_mod)
                    v.scalar_tensor_tensor(gain[:, :], mod[:, shift0 + KC:shift0 + 2 * KC], 1.0, gains,
                                           ALU.add, ALU.mult).then_inc(gain_ready, 1)
                    dve.wait_ge(gain_ready, i + 1)
                if i:
                    inverse_rms(i)
                inv_all = inv[:, :].rearrange("p (o t) -> p o t", o=1).broadcast_to([P, EK, T])
                for e in range(NE):
                    if e >= WR:
                        dve.wait_ge(*((out_turned, e // 2 - 1) if gains is None else (h_ready, NE * i + e - WR + 1)))
                    v.tensor_tensor(pair(e), xT[:, EK * e:EK * (e + 1), :], inv_all, ALU.mult).then_inc(scaled, 1)
                    if gains is not None and e:
                        low(i, e - 1)
                    dve.wait_ge(scaled, NE * i + e + 1)
                    for j in range(EK):
                        k = EK * e + j
                        if gains is None:
                            v.tensor_scalar(pair(e)[:, j, :], pair(e)[:, j, :], vcol[:, 0, 5 * KC + k:5 * KC + k + 1],
                                            None, ALU.mult).then_inc(modulated, 1)
                        else:
                            v.tensor_scalar(pair(e)[:, j, :], pair(e)[:, j, :], gain[:, k:k + 1],
                                            mod[:, shift0 + k:shift0 + k + 1], ALU.mult, ALU.add).then_inc(modulated, 1)
                if gains is not None:
                    low(i, NE - 1)
                    dve.wait_ge(h_ready, NE * (i + 1))

            def low(i, e):
                dve.wait_ge(h_hi, NE * i + e + 1)
                v.tensor_tensor(h[:, EK * e:EK * (e + 1), 1, :], pair(e), h[:, EK * e:EK * (e + 1), 0, :].bitcast(F32),
                                ALU.subtract).then_inc(h_ready, 1)

            norm(0, MIX_GAIN[0], 0, A_START)
            for e in range(WR):
                split(0, e)
            dve.wait_ge(f_done, 1)
            v.tensor_tensor(fz[:, :, :], ps[:, NB + 1:NB + 1 + TT, 0:H],
                            bf[:, :].rearrange("p (o h) -> p o h", o=1).broadcast_to([P, TT, H]), ALU.add).then_inc(f_step, 1)
            dve.wait_ge(f_step, 1)
            v.scalar_tensor_tensor(fe[:, :, :], fz[:, :, :], -1.0, fz[:, :, :], ALU.mult, ALU.min).then_inc(f_step, 1)
            dve.wait_ge(f_act, 2)
            v.scalar_tensor_tensor(log_f[:, :, :], fz[:, :, :], 0.0, fe[:, :, :], ALU.min, ALU.subtract).then_inc(f_step, 1)

            def forget_rows():
                dve.wait_ge(f_act, 3)
                v.scalar_tensor_tensor(nf_lo[:, :], ps[0:H, 1, 0:T], -1.0, nf_hi[:, :].bitcast(F32),
                                       ALU.mult, ALU.subtract).then_inc(f_rows, 1)
                v.tensor_copy(f_tok[:, :, :], ps[:, 2, 0:TT * H].rearrange("p (a h) -> p a h", a=TT)).then_inc(f_rows, 1)

            def maxima(g, s_bank):
                f_g = f_tok[:, :, NB * g:NB * (g + 1)]
                dve.wait_ge(scores_done, g + 1)
                for b in range(TT):
                    v.tensor_reduce(row_max[:, b, :], ps[:, s_bank:s_bank + NB, P * b:P * b + P * (b + 1)], AX.X,
                                    ALU.max).then_inc(max_step, 1)
                dve.wait_ge(max_step, 4 * g + 2)
                dve.wait_ge(f_rows, 2)
                v.tensor_tensor(row_max[:, :, :], row_max[:, :, :], f_g, ALU.add).then_inc(max_step, 1)
                dve.wait_ge(max_step, 4 * g + 3)
                v.tensor_tensor(exp_bias[:, :, :], f_g, row_max[:, :, :], ALU.subtract).then_inc(max_step, 1)

            def normalise(g):
                dve.wait_ge(exp_done, 8 * g + 8)
                v.reciprocal(row_inv[:, :, :], row_sum[:, :, :]).then_inc(norm_p, 1)
                dve.wait_ge(norm_p, 3 * g + 1)
                for b, pr in enumerate((prob0, prob1)):
                    n = P * (b + 1)
                    v.tensor_tensor(pr, pr, row_inv[:, b, :].rearrange("p (j o) -> p j o", o=1).broadcast_to([P, NB, n]),
                                    ALU.mult).then_inc(norm_p, 1)

            def low_probs(g, s_bank):
                dve.wait_ge(pt_hi_ready, g + 1)
                v.tensor_tensor(pt_lo, ps[:, s_bank:s_bank + NB, 0:T + P], pt_hi.bitcast(F32), ALU.subtract).then_inc(pt_ready, 1)

            def low_attn(g, o_bank):
                dve.wait_ge(attn_hi, g + 1)
                v.tensor_tensor(mid[:, NB * g:NB * (g + 1), 1, :],
                                ps[:, o_bank:o_bank + 2, :].rearrange("p b (j t) -> p (b j) t", j=2),
                                mid[:, NB * g:NB * (g + 1), 0, :].bitcast(F32), ALU.subtract).then_inc(attn_ready, 1)

            for g in range(NG):
                for t in range(3):
                    u = 3 * g + t
                    par = u % 2

                    def evac():
                        if t == 2:
                            dve.wait_ge(qkv_hi, 3 * g + 3)
                            v.tensor_tensor(vs[:, :, 1, :], ps[:, NB * par:NB * par + TT, :],
                                            vs[:, :, 0, :].bitcast(F32), ALU.subtract).then_inc(evacuated, 1)
                        else:
                            dst = (qs, ks)[t]
                            whole(u, par, fsum, SCALE if t == 0 else 1.0, n_half=2 * g + t + 1,
                                  used=((qkv_ready, 2 * g + t),))
                            dve.wait_ge(qkv_hi, 3 * g + t + 1)
                            v.tensor_tensor(dst[:, :, 1, :], fsum, dst[:, :, 0, :].bitcast(F32), ALU.subtract).then_inc(qkv_ready, 1)
                    after = None
                    if t == 0 and g:
                        after = {1: lambda: low_attn(g - 1, NB * (1 - par) + 2)}
                    elif t == 1 and g == 0:
                        after = {1: forget_rows}
                    elif t == 2:
                        after = {0: lambda: maxima(g, NB * (1 - par)), 1: lambda: normalise(g),
                                 2: lambda: low_probs(g, NB * (1 - par))}
                    body(u, evac, (u + A_START, par),
                         (u + A_START - 1, NB * par + NB - 1 if t == 2 else NB * (1 - par)) if u else None, after=after,
                         ada_first=t == 2, ada_late=2 if t == 1 else NQ)
            for n in range(NG):
                u = U_OUT0 + n
                body(u, lambda: residual(u, n % 2, NB * n, n, u - NG + 1, n),
                     (u + A_START, n % 2), (u + A_START - 1, NB * ((n + 1) % 2)),
                     after=None if n else {1: lambda: low_attn(NG - 1, NB + 2)})

            def mlp_slice(s, base, l, adas, last=False):
                n_hid = SLICES * NG * l + NG * s
                n_add = NG * (1 + l) + n_hid
                for n in range(2 * NG):
                    u = base + 2 * NG * s + n
                    a = A_MLP0 + NG * s + n // 2

                    def evac():
                        if n >= NG:
                            residual(u, n % 2, NB * (n - NG), n - NG, u - NG + 1, n_add + n - NG, ((hid_ready, n_hid + NG),))
                            return
                        whole(u, n % 2, fsum, n_half=u - NG + 1, used=((hid_ready, n_hid + n), (added, n_add)))
                        dve.wait_ge(evacuated, u + 3)
                        v.scalar_tensor_tensor(fsum, fsum, 0.0, fsum, ALU.max, ALU.mult).then_inc(relu2, 1)
                        dve.wait_ge(hid_hi, n_hid + n + 1)
                        v.tensor_tensor(mid[:, NB * n:NB * (n + 1), 1, :], fsum,
                                        mid[:, NB * n:NB * (n + 1), 0, :].bitcast(F32), ALU.subtract).then_inc(hid_ready, 1)
                    body(u, evac, (a, (n // 2) % 2) if adas else None,
                         (a - 1, NB * ((n + 1) % 2)) if adas and n % 2 == 0 else None,
                         more=not (last and n == 2 * NG - 1),
                         ada_q=(2, None, 3, None) if n % 2 else (0, None, 1, None))

            norm(1, MLP_GAIN[0], 3 * KC, A_MLP0 - 1)
            with dve.Fori(0, SLICES) as s:
                mlp_slice(s, U_MLP0, 0, True)
            ada_store(A_CONV - 1, 0)
            norm(2, MIX_GAIN[1], NROW, A_CONV)
            v.memset(conv_u[:, :, 0:2], 0.0).then_inc(conv_zero, 1)
            dve.wait_ge(conv_zero, 1)
            with dve.Fori(0, NG // 2) as r:
                for i in range(2):
                    g = 2 * r + i
                    for t in range(3):
                        pos = 3 * i + t
                        u = U_CONV + 6 * r + pos
                        a = A_CONV + 4 * r + 2 * i + t

                        def evac():
                            whole(u, pos % 2, (conv_b[:, :, :], conv_c[:, :, :], fsum)[t], n_half=u - NG + 1)
                            if t == 2:
                                dve.wait_ge(evacuated, u + 3)
                                v.tensor_tensor(conv_u[:, :, 2:T + 2], conv_c[:, :, :], fsum, ALU.mult).then_inc(conv_in, 1)
                                dve.wait_ge(conv_in, g + 1)
                                dve.wait_ge(conv_tap, g + 1)
                                for tap in (1, 2):
                                    for j in range(NB):
                                        v.scalar_tensor_tensor(
                                            conv_y[:, j, :], conv_u[:, j, tap:tap + T], taps[:, ds(KC * tap + NB * g + j, 1)],
                                            conv_y[:, j, :], ALU.mult, ALU.add).then_inc(conv_step, 1)
                                    dve.wait_ge(conv_step, 2 * NB * g + NB * tap)
                                v.tensor_tensor(conv_y[:, :, :], conv_b[:, :, :], conv_y[:, :, :], ALU.mult).then_inc(conv_gated, 1)
                                dve.wait_ge(conv_hi, g + 1)
                                v.tensor_tensor(mid[:, ds(NB * g, NB), 1, :], conv_y[:, :, :],
                                                mid[:, ds(NB * g, NB), 0, :].bitcast(F32), ALU.subtract).then_inc(conv_ready, 1)
                        body(u, evac, (a, t % 2) if t < 2 else None, (a - 1, NB * ((pos + 1) % 2)) if t else None)
            for n in range(NG):
                u = U_OUT1 + n
                body(u, lambda: residual(u, n % 2, NB * n, n, u - NG + 1, NG * (1 + SLICES) + n))
            norm(3, MLP_GAIN[1], NROW + 3 * KC, A_END)
            with dve.Fori(0, SLICES - 1) as s:
                mlp_slice(s, U_MLP1, 1, False)
            mlp_slice(SLICES - 1, U_MLP1, 1, False, last=True)
            norm(4)
            for m in range(NG):
                dve.wait_ge(out_turned, m + 1)
                v.tensor_copy(raw[:, m, 1, :], ps[:, NB + 2 * (m % 2) + 1, :]).then_inc(out_copied1, 1)


_INS = ['x', 'c', 'ada_w', 'ada_b', 'norm_mix', 'norm_mlp', 'fox_w_in', 'fox_b_f', 'fox_w_out', 'conv_w_in',
        'conv_w', 'conv_w_out', 'mlp_w_up', 'mlp_w_down', 'final_norm']


def kernel(**inputs):
    import numpy as _np
    import concourse.bacc as _bacc
    from concourse import mybir as _mybir
    from concourse.bass_utils import run_bass_kernel_spmd as _run

    nc = _bacc.Bacc("TRN2", target_bir_lowering=False, num_devices=1)
    arrays, args = {}, []
    for name in _INS:
        a = _np.ascontiguousarray(inputs[name])
        arrays[f"in_{name}_dram"] = a
        args.append(nc.dram_tensor(f"in_{name}_dram", a.shape, _mybir.dt.from_np(a.dtype), kind="ExternalInput").ap())
    args.append(nc.dram_tensor("out_dram", (1, T, D), F32, kind="ExternalOutput").ap())
    build(nc, *args)
    r = _run(nc, [arrays], core_ids=[0])
    return r.results[0]["out_dram"]
```
